# Optimizing a Trainium2 kernel written in Bass

```python
import jax, jax.numpy as jnp
from jax import lax
import numpy as np

D_MODEL = 2048
BATCH = 1
SEQ = 512
DEPTH = 1

MIX_WIDTH = D_MODEL
GLA_HEADS = 4
GLA_DV = MIX_WIDTH // 2 // GLA_HEADS
GLA_DK = GLA_DV // 2
GLA_RANK = 16
GLA_TAU = 16.0
GLA_CHUNK = 64
ATT_HEADS = 16
ATT_HD = (MIX_WIDTH - GLA_HEADS * GLA_DV) // ATT_HEADS
DILATED_PATTERNS = ((128, 1), (512, 4), (2048, 16))
PEER_NKEYS = 128
PEER_EXPERTS = PEER_NKEYS * PEER_NKEYS
PEER_HEADS = 8
PEER_TOPK = 16
PEER_DQ = 256
PEER_TOKEN_BLOCK = 64
EPS = 1e-6
NEG = -1e30

GLA_QK = GLA_HEADS * GLA_DK
GLA_V = GLA_HEADS * GLA_DV
ATT_W = ATT_HEADS * ATT_HD
IN_SPLITS = (GLA_QK, GLA_QK, GLA_V, GLA_V, GLA_RANK, GLA_RANK, ATT_W, ATT_W, ATT_W)
IN_WIDTH = sum(IN_SPLITS)

kernel_name = "hymba_gla_dilated_peer_encoder"

def rms_norm(x, g):
    xf = x.astype(jnp.float32)
    y = xf * lax.rsqrt(jnp.mean(xf * xf, axis=-1, keepdims=True) + EPS)
    return (y * g.astype(jnp.float32)).astype(x.dtype)

def alibi_slopes(n):
    return (2.0 ** (-8.0 * np.arange(1, n + 1) / n)).astype(np.float32)

def gla_chunked(q, k, v, log_a):
    B, H, S, dk = q.shape
    dv = v.shape[-1]
    C = GLA_CHUNK
    N = S // C
    q = q.reshape(B, H, N, C, dk)
    k = k.reshape(B, H, N, C, dk)
    v = v.reshape(B, H, N, C, dv)
    b = jnp.cumsum(log_a.reshape(B, H, N, C, dk), axis=3)
    b_last = b[:, :, :, -1:, :]
    q_d = q * jnp.exp(b)
    k_d = k * jnp.exp(-b)
    causal = jnp.tril(jnp.ones((C, C), dtype=bool))
    att = jnp.where(causal, jnp.einsum('bhncd,bhnsd->bhncs', q_d, k_d), 0.0)
    o_intra = jnp.einsum('bhncs,bhnse->bhnce', att, v)
    kv = jnp.einsum('bhncd,bhnce->bhnde', k * jnp.exp(b_last - b), v)
    decay = jnp.exp(b_last[:, :, :, 0, :])

    def step(state, inp):
        dec, kv_n = inp
        return dec[..., None] * state + kv_n, state

    init = jnp.zeros((B, H, dk, dv), q.dtype)
    _, prev = lax.scan(step, init, (jnp.moveaxis(decay, 2, 0), jnp.moveaxis(kv, 2, 0)))
    prev = jnp.moveaxis(prev, 0, 2)
    o_inter = jnp.einsum('bhncd,bhnde->bhnce', q_d, prev)
    return (o_intra + o_inter).reshape(B, H, S, dv)

def dilated_band(q, k, v, slopes, dilation, radius):
    B, H, S, hd = q.shape
    L = S // dilation
    blk = radius
    nb = -(-L // blk)
    Lp = nb * blk

    def to_sub(t):
        return t.reshape(B, H, L, dilation, hd).transpose(0, 1, 3, 2, 4)

    qs = jnp.pad(to_sub(q), ((0, 0),) * 3 + ((0, Lp - L), (0, 0))).reshape(B, H, dilation, nb, blk, hd)
    pad_kv = ((0, 0),) * 3 + ((blk, Lp - L + blk), (0, 0))

    def windows(t):
        t = jnp.pad(to_sub(t), pad_kv).reshape(B, H, dilation, nb + 2, blk, hd)
        return jnp.concatenate([t[:, :, :, :-2], t[:, :, :, 1:-1], t[:, :, :, 2:]], axis=4)

    kw, vw = windows(k), windows(v)
    q_pos = jnp.arange(nb)[:, None] * blk + jnp.arange(blk)[None, :]
    k_pos = jnp.arange(nb)[:, None] * blk - blk + jnp.arange(3 * blk)[None, :]
    off = k_pos[:, None, :] - q_pos[:, :, None]
    valid = (jnp.abs(off) <= radius) & (k_pos[:, None, :] >= 0) & (k_pos[:, None, :] < L)
    dist = (jnp.abs(off) * dilation).astype(jnp.float32)
    s = jnp.einsum('bhrnqd,bhrnkd->bhrnqk', qs, kw)
    s = s - slopes[None, :, None, None, None, None] * dist
    s = jnp.where(valid, s, NEG)
    m = jnp.max(s, axis=-1)
    p = jnp.exp(s - m[..., None])
    l = jnp.sum(p, axis=-1)
    num = jnp.einsum('bhrnqk,bhrnkd->bhrnqd', p, vw)

    def from_sub(t):
        t = t.reshape((B, H, dilation, Lp) + t.shape[5:])[:, :, :, :L]
        t = jnp.moveaxis(t, 2, 3)
        return t.reshape((B, H, S) + t.shape[4:])

    return from_sub(num), from_sub(m), from_sub(l)

def hybrid_mixer(h, w_in, gate_up_f, gate_bias_f, gate_up_b, gate_bias_b, gla_norm_g, att_norm_g, w_out):
    B, S, _ = h.shape
    f32 = jnp.float32
    proj = jnp.einsum('bsd,de->bse', h, w_in)
    offsets = [int(o) for o in np.cumsum(IN_SPLITS)[:-1]]
    gq, gk, gv, gr, gdf, gdb, aq, ak, av = jnp.split(proj, offsets, axis=-1)

    def heads(t, n):
        return t.reshape(B, S, n, -1).transpose(0, 2, 1, 3).astype(f32)

    q = heads(gq, GLA_HEADS) * (GLA_DK ** -0.5)
    k = heads(gk, GLA_HEADS)
    v = heads(gv, GLA_HEADS)

    def log_gate(down, up, bias):
        z = (jnp.einsum('bsr,rk->bsk', down, up) + bias).astype(f32)
        return heads(jax.nn.log_sigmoid(z) / GLA_TAU, GLA_HEADS)

    la_f = log_gate(gdf, gate_up_f, gate_bias_f)
    la_b = log_gate(gdb, gate_up_b, gate_bias_b)
    flip = lambda t: jnp.flip(t, axis=2)
    o_f = gla_chunked(q, k, v, la_f)
    o_b = flip(gla_chunked(flip(q), flip(k), flip(v), flip(la_b)))
    o = rms_norm(o_f + o_b, gla_norm_g)
    o = o.transpose(0, 2, 1, 3).reshape(B, S, GLA_V)
    gla_out = o * jax.nn.silu(gr.astype(f32))

    q = heads(aq, ATT_HEADS) * (ATT_HD ** -0.5)
    k = heads(ak, ATT_HEADS)
    v = heads(av, ATT_HEADS)
    slopes = jnp.asarray(alibi_slopes(ATT_HEADS))
    nums, maxs, dens = [], [], []
    for window, dilation in DILATED_PATTERNS:
        n_, m_, l_ = dilated_band(q, k, v, slopes, dilation, window // (2 * dilation))
        nums.append(n_); maxs.append(m_); dens.append(l_)
    nums, maxs, dens = jnp.stack(nums), jnp.stack(maxs), jnp.stack(dens)
    w = jnp.exp(maxs - jnp.max(maxs, axis=0, keepdims=True))
    att = jnp.sum(w[..., None] * nums, axis=0) / jnp.sum(w * dens, axis=0)[..., None]
    att = att.transpose(0, 2, 1, 3).reshape(B, S, ATT_W)
    att = rms_norm(att, att_norm_g)

    y = jnp.concatenate([gla_out, att], axis=-1).astype(h.dtype)
    return jnp.einsum('bse,ed->bsd', y, w_out)

def peer_ffn(h, w_q, sub_keys, expert_u, expert_v):
    B, S, D = h.shape
    T = B * S
    f32 = jnp.float32
    x = h.reshape(T, D)
    q = jnp.einsum('td,de->te', x, w_q).reshape(T, PEER_HEADS, 2, PEER_DQ // 2).astype(f32)
    s = jnp.einsum('thcd,hckd->thck', q, sub_keys.astype(f32))
    sc, si = lax.top_k(s, PEER_TOPK)
    cand = (sc[:, :, 0, :, None] + sc[:, :, 1, None, :]).reshape(T, PEER_HEADS, PEER_TOPK * PEER_TOPK)
    top_sc, top_ci = lax.top_k(cand, PEER_TOPK)
    i1 = jnp.take_along_axis(si[:, :, 0], top_ci // PEER_TOPK, axis=-1)
    i2 = jnp.take_along_axis(si[:, :, 1], top_ci % PEER_TOPK, axis=-1)
    experts = i1 * PEER_NKEYS + i2
    gates = jax.nn.softmax(top_sc, axis=-1)
    TB = PEER_TOKEN_BLOCK
    nblk = T // TB

    def block(args):
        xb, eb, gb = args
        a = jax.nn.gelu(jnp.einsum('td,thkd->thk', xb, expert_u[eb]).astype(f32), approximate=False)
        wgt = (gb * a).astype(xb.dtype)
        return jnp.einsum('thk,thkd->td', wgt, expert_v[eb])

    out = lax.map(block, (x.reshape(nblk, TB, D),
                          experts.reshape(nblk, TB, PEER_HEADS, PEER_TOPK),
                          gates.reshape(nblk, TB, PEER_HEADS, PEER_TOPK)))
    return out.reshape(B, S, D).astype(h.dtype)

def setup_inputs(seed: int = 0) -> dict:
    key = jax.random.key(seed)
    ks = jax.random.split(key, 20)
    nrm = lambda k, shape, scale: jax.random.normal(k, shape, jnp.float32) * scale
    L = DEPTH
    return {
        "x": nrm(ks[0], (BATCH, SEQ, D_MODEL), 1.0),
        "norm1_g": 1.0 + nrm(ks[1], (L, D_MODEL), 0.02),
        "w_in": nrm(ks[2], (L, D_MODEL, IN_WIDTH), D_MODEL ** -0.5),
        "gla_gate_up_f": nrm(ks[3], (L, GLA_RANK, GLA_QK), GLA_RANK ** -0.5),
        "gla_gate_bias_f": nrm(ks[4], (L, GLA_QK), 0.1),
        "gla_gate_up_b": nrm(ks[5], (L, GLA_RANK, GLA_QK), GLA_RANK ** -0.5),
        "gla_gate_bias_b": nrm(ks[6], (L, GLA_QK), 0.1),
        "gla_norm_g": 1.0 + nrm(ks[7], (L, GLA_DV), 0.02),
        "att_norm_g": 1.0 + nrm(ks[8], (L, ATT_W), 0.02),
        "w_out": nrm(ks[9], (L, MIX_WIDTH, D_MODEL), MIX_WIDTH ** -0.5),
        "norm2_g": 1.0 + nrm(ks[10], (L, D_MODEL), 0.02),
        "peer_w_q": nrm(ks[11], (L, D_MODEL, PEER_HEADS * PEER_DQ), D_MODEL ** -0.5),
        "peer_sub_keys": nrm(ks[12], (L, PEER_HEADS, 2, PEER_NKEYS, PEER_DQ // 2), (PEER_DQ // 2) ** -0.5),
        "peer_u": nrm(ks[13], (L, PEER_EXPERTS, D_MODEL), D_MODEL ** -0.5),
        "peer_v": nrm(ks[14], (L, PEER_EXPERTS, D_MODEL), 0.5),
        "final_norm_g": 1.0 + nrm(ks[15], (D_MODEL,), 0.02),
    }

def reference(x, norm1_g, w_in, gla_gate_up_f, gla_gate_bias_f, gla_gate_up_b, gla_gate_bias_b,
              gla_norm_g, att_norm_g, w_out, norm2_g, peer_w_q, peer_sub_keys, peer_u, peer_v,
              final_norm_g):
    for l in range(DEPTH):
        h = x + hybrid_mixer(rms_norm(x, norm1_g[l]), w_in[l], gla_gate_up_f[l], gla_gate_bias_f[l],
                             gla_gate_up_b[l], gla_gate_bias_b[l], gla_norm_g[l], att_norm_g[l], w_out[l])
        x = h + peer_ffn(rms_norm(h, norm2_g[l]), peer_w_q[l], peer_sub_keys[l], peer_u[l], peer_v[l])
    return rms_norm(x, final_norm_g)


_drawn_inputs = setup_inputs


def setup_inputs(seed=0):
    import zlib

    import numpy as np

    out = dict(_drawn_inputs(seed))
    spreads = {}
    factors = {}
    for name, (base, spread) in spreads.items():
        noise = np.random.default_rng([zlib.crc32(name.encode()), seed]).standard_normal(out[name].shape)
        drawn = base * np.exp(spread * noise) if base else spread * noise
        out[name] = __import__('jax').numpy.asarray(drawn.astype(out[name].dtype))
    for name, factor in factors.items():
        out[name] = (out[name] * factor).astype(out[name].dtype)
    return out
```

```python
from collections import namedtuple
from contextlib import ExitStack

import concourse.bass as bass
import numpy as np
from concourse import mybir

F32 = mybir.dt.float32
U8 = mybir.dt.uint8
F32R = mybir.dt.float32r
U32 = mybir.dt.uint32
ALU = mybir.AluOpType
ACT = mybir.ActivationFunctionType
AX = mybir.AxisListType

P = 128
T = 512
TT = T // P
D = 2048
KD = D // P
GLA_HEADS, DK, DV, RANK, CHUNK = 4, 128, 256, 16, 64
NC = T // CHUNK
DVT = DV // P
ATT_HEADS, HD = 16, 64
NKEYS, PEER_HEADS, TOPK = 128, 8, 16
EPS = 1e-6
TAU = 16.0
PATTERNS = ((128, 1), (512, 4), (2048, 16))
NEG = -1e30
LOW = -3.0e38

JOB_GATE = 0
GROUP = 6
NGLA = GLA_HEADS
NATT = ATT_HEADS // 4
JOB_GROUPS = 1
JOB_OUT = JOB_GROUPS + GROUP * (NGLA + NATT)
JOB_Q = JOB_OUT + KD
JOB_U = JOB_Q + 2 * PEER_HEADS
NJOBS = JOB_U + NKEYS
PARTS = 3 * GROUP
CUT = (0, 6, 11, KD)

V_N1, V_N2, V_NF, V_ATT, V_GLA, V_BIAS, V_SLOPE = 0, KD, 2 * KD, 3 * KD, 3 * KD + 8, 3 * KD + 10, 3 * KD + 18
NVEC = V_SLOPE + ATT_HEADS

VEC_TOP = 52
BANKS_FREE, HOT_FREE = 4, 2
KV_BANKS = (2, 3, 4, 7)
VEC_GLA, VEC_ATT = 8, 34
U1 = 16
U2 = 16
TB = T // U2
VG = 4
VR = NKEYS // VG
HALF = D // 2
HT = HALF // P

Job = namedtuple("Job", "n slot use")


def job(first, per, i, j):
    slot = (first + j) % 2
    return Job(first + per * i + j, slot, (first + j - slot) // 2 + (per // 2) * i)


class Chain:

    def __init__(self, eng, sem):
        self.eng, self.sem, self.n, self.base = eng, sem, 0, 0

    def __call__(self, ins):
        self.n += 1
        ins.then_inc(self.sem, 1)
        self.eng.wait_ge(self.sem, self.base + self.n)

    def enter(self, i, per):
        self.outer, self.per = (self.base, self.n), per
        self.base, self.n = self.base + self.n + i * per, 0

    def leave(self, rounds):
        assert self.n == self.per, (self.n, self.per)
        self.base, self.n = self.outer[0], self.outer[1] + rounds * self.per


def layer(nc, x_t, weights, peer_v, sub_keys, vectors, gate_up, dist, count, ident, scan_mask, steps, out_t):
    with ExitStack() as ctx:
        def sb(name, shape, dt=F32):
            return ctx.enter_context(nc.sbuf_tensor(name, shape, dt))

        def sem(name):
            return ctx.enter_context(nc.semaphore(name))

        psum = ctx.enter_context(nc.psum_tensor("psum", [P, 8, T], F32))
        act_hi, act_lo = sb("act_hi", [P, KD, T], F32R), sb("act_lo", [P, KD, T], F32R)
        raw = sb("raw", [P, 2, KD, P])
        w_hi, w_lo = sb("w_hi", [P, 2, KD, P], F32R), sb("w_lo", [P, 2, KD, P], F32R)
        cur = sb("cur", [P, KD, T])
        work = sb("work", [P, 28, T])
        vec = sb("vec", [P, NVEC])
        ones, idn = sb("ones", [P, P]), sb("idn", [P, P])
        small = sb("small", [P, 64])

        h_dram = nc.dram_tensor("h_dram", [P, KD, T], F32, kind="Internal").ap()
        gelu_dram = nc.dram_tensor("gelu_dram", [NKEYS, P, T], F32, kind="Internal").ap()
        gate_dram = nc.dram_tensor("gate_dram", [U2, P, NKEYS * TB], F32, kind="Internal").ap()

        s_raw = [sem("s_raw0"), sem("s_raw1")]
        s_hi, s_lo = sem("s_hi"), sem("s_lo")
        s_jobmm, s_jobev = sem("s_jobmm"), sem("s_jobev")
        s_const, s_ones, s_mask = sem("s_const"), sem("s_ones"), sem("s_mask")
        s_x = [sem(f"s_x{q}") for q in range(4)]
        s_sq, s_ssmm, s_rinv, s_r = sem("s_sq"), sem("s_ssmm"), sem("s_rinv"), sem("s_r")
        s_n, s_nhi, s_nlo = sem("s_n"), sem("s_nhi"), sem("s_nlo")
        s_vec, s_act = sem("s_vec"), sem("s_act")
        s_take = sem("s_take")
        s_up, s_z, s_zb, s_ln, s_cum, s_exc, s_e, s_dec = [sem(n) for n in (
            "s_up", "s_z", "s_zb", "s_ln", "s_cum", "s_exc", "s_e", "s_dec")]
        s_qk, s_vtp, s_vt, s_att, s_ate, s_atm, s_ats, s_ktp, s_kt = [sem(n) for n in (
            "s_qk", "s_vtp", "s_vt", "s_att", "s_ate", "s_atm", "s_ats", "s_ktp", "s_kt")]
        s_kv, s_st, s_o, s_osq, s_oss, s_ginv, s_gr, s_sil, s_y = [sem(n) for n in (
            "s_kv", "s_st", "s_o", "s_osq", "s_oss", "s_ginv", "s_gr", "s_sil", "s_y")]
        s_tab = sem("s_tab")
        s_avp, s_av, s_qkm, s_sb, s_p, s_ptp, s_pt, s_pv, s_nrm, s_otp, s_ot = [sem(n) for n in (
            "s_avp", "s_av", "s_qkm", "s_sb", "s_p", "s_ptp", "s_pt", "s_pv", "s_nrm", "s_otp", "s_ot")]
        s_xr, s_hsaved = [sem("s_xr0"), sem("s_xr1")], sem("s_hsaved")
        s_keys, s_scp, s_sc = sem("s_keys"), sem("s_scp"), sem("s_sc")
        s_apart = sem("s_apart")
        s_tke, s_tkx, s_route, s_rtp, s_rt = sem("s_tke"), sem("s_tkx"), sem("s_route"), sem("s_rtp"), sem("s_rt")
        s_gst, s_gd = [sem(f"s_gst{n}") for n in range(4)], [sem(f"s_gd{n}") for n in range(2)]
        s_hot, s_gmm, s_gev = sem("s_hot"), sem("s_gmm"), sem("s_gev")
        s_v, s_a, s_g = [sem(f"s_v{n}") for n in range(VG)], [sem(f"s_a{n}") for n in range(VG)], [sem("s_g0"), sem("s_g1")]
        s_vh, s_vl, s_w, s_wh, s_wl, s_vmm = [sem(n) for n in ("s_vh", "s_vl", "s_w", "s_wh", "s_wl", "s_vmm")]
        s_hl, s_vend, s_vev, s_fin, s_out = sem("s_hl"), sem("s_vend"), sem("s_vev"), sem("s_fin"), sem("s_out")

        block = ctx.enter_context(nc.Block())

        up, gates_in = sb("up", [32 + RANK, DK]), sb("gates_in", [P, T])
        gd, gup = gates_in[0:32 + RANK], gates_in[64:96 + RANK]
        bias, dec, slope = small[:, 0:2], small[:, 2:18].rearrange("p (d n) -> p d n", d=2), small[:, 18:22]
        negmax, rden = small[:, 22:24], small[:, 24:25]

        fresh, taken = work[:, 0:6], work[:, 6:12]
        n_tmp, sq_tmp, r_t, ri_t = work[:, 0:2], work[:, 2:4], work[:, 4], work[:, 5]
        zb, ab, la, cum, exc = [work[:, 12 + n] for n in range(5)]
        qd, kd, ke, mask = work[:, 17:19], work[:, 19:21], work[:, 21], work[:, 22]
        kt = work[:, 23:25]
        vt = work[:, 25:27].rearrange("p a (b e) -> p (a b) e", e=DV)
        at = work[:, 27].rearrange("p (d a c) -> p d a c", d=2, c=CHUNK)
        at_sum = sb("at_sum", [P, NC // 2, P])
        osq, sil, g_r, g_ri = work[:, 19:21], work[:, 12:14], work[:, 14], work[:, 15]
        state = cur[:, 8:16]
        logit, prob, prob_t = work[:, 12:14], work[:, 14:16], work[:, 16:18]
        dist_t = work[:, 18:22]
        count_t = work[:, 22].bitcast(U8).rearrange("p (b t) -> p b t", t=T)
        va = work[:, 24:27].rearrange("p a b -> p (a b)")[:, 0:16 * (HD + 1)].rearrange(
            "p (r s h e) -> p r s h e", r=2, s=TT, h=2)
        att_rows = work[:, 27].rearrange("p (a e) -> p a e", e=P)
        x_res = work[:, 12:14]
        q_t, keys = work[:, 14:16], work[:, 16:20].rearrange("p a b -> p (a b)").rearrange("p (n k) -> p n k", k=NKEYS)
        score_t = cur[:, :].rearrange("p a b -> p (a b)")
        gelu_t = work[:, 0:4]
        tk_in, tk_cut = [work[:, 4, 256 * n:256 * n + 256].rearrange("p (c k) -> p c k", c=2) for n in range(2)]
        pair_sum, pair_cut = work[:, 5, 0:256], work[:, 5, 256:512]
        picked, chosen = [work[:, 6, 256 * n:256 * n + 256].rearrange("p (a b) -> p a b", b=TOPK) for n in range(2)]
        tiny = work[:, 7].rearrange("p (n k) -> p n k", k=TOPK)
        val, idx, idx_f = tiny[:, 0:2], tiny[:, 2:4].bitcast(U32), tiny[:, 4:6]
        top, place, place_2, place_f = tiny[:, 6:8], tiny[:, 8].bitcast(U32), tiny[:, 9:11].bitcast(U32), tiny[:, 11:13]
        top_exp, tk_neg, tk_sum, tk_inv = tiny[:, 13:15], tiny[:, 15, 0:2], tiny[:, 15, 2:4], tiny[:, 15, 4:6]
        count_up = work[:, 8, 0:NKEYS]
        routed = work[:, 9:12]
        routed_t = work[:, 12:15]
        hot2 = work[:, 15:17].rearrange("p a b -> p (a b)").rearrange("p (n k) -> p n k", k=NKEYS)
        hot1 = work[:, 17:19].rearrange("p a b -> p (a b)").rearrange("p (n k) -> p n k", k=NKEYS)
        route_tb = work[:, 19, 0:6 * TB].rearrange("p (r x t) -> p r x t", r=2, x=3)
        gate_t = cur[:, :].rearrange("p (r a) t -> p r (a t)", r=2).rearrange("p r (i t) -> p r i t", t=TB)
        g_t = work[:, 0:8].rearrange("p (r a) t -> p r (a t)", r=2).rearrange("p r (b e t) -> p r b e t", b=U2, e=VG)
        a_t, weight_t = work[:, 8:12], work[:, 16:18]
        v_raw = work[:, 20:28].rearrange("p a t -> p (a t)").rearrange("p (n c) -> p n c", c=HALF)
        v_hi, v_lo = [x[:, :, :].rearrange("p a t -> p (a t)").rearrange("p (n c) -> p n c", c=HALF) for x in (act_hi, act_lo)]
        g_hi, g_lo = [x[:, :, :, :].rearrange("p s k c -> p (s k c)").rearrange("p (n t) -> p n t", t=T) for x in (w_hi, w_lo)]

        @block.sync
        def _(sp):
            for n in range(2):
                sp.dma_start(raw[:, n], weights[n].rearrange("p (k c) -> p k c", c=P)).then_inc(s_raw[n], 16)
            last = NJOBS
            with sp.Fori(0, (last - 3) // 2) as i:
                for j in range(2):
                    J = job(2, 2, i, j)
                    sp.wait_ge(s_lo, J.n - 1)
                    sp.dma_start(raw[:, J.slot], weights[bass.ds(J.n, 1)].rearrange("o p (k c) -> p (o k) c", c=P)
                                 ).then_inc(s_raw[J.slot], 16)
            for n in range(2 + 2 * ((last - 3) // 2), last):
                sp.wait_ge(s_lo, n - 1)
                sp.dma_start(raw[:, n % 2], weights[n].rearrange("p (k c) -> p k c", c=P)).then_inc(s_raw[n % 2], 16)


            def v_tile(half, i, r, e, early):
                n = NKEYS * half + 8 * i + 4 * r + e
                if not early:
                    sp.wait_ge(s_vl, n - 3)
                rows = bass.ds(8 * i + 4 * r + e, 1)
                sp.dma_start(v_raw[:, e], peer_v.rearrange("(m p) d -> m p d", p=P)[rows, :, HALF * half:HALF * (half + 1)]
                             .rearrange("o p d -> p (o d)")).then_inc(s_v[e], 16)

            def w_tiles(half, i, r, first):
                n = NKEYS * half + 8 * i + 4 * r
                if not first:
                    sp.wait_ge(s_w, n - 4)
                m = (8 * i + 4 * r) * TB
                sp.dma_start(g_t[:, r].rearrange("p b e t -> p b (e t)"),
                             gate_dram[:, :, bass.ds(m, VG * TB)].rearrange("b p c -> p b c")).then_inc(s_g[r], 16)

            def a_tile(half, i, r, e, first):
                n = NKEYS * half + 8 * i + 4 * r + e
                if not first:
                    sp.wait_ge(s_w, n - 3)
                sp.dma_start(a_t[:, e], gelu_dram[bass.ds(8 * i + 4 * r + e, 1)].rearrange("o p t -> p (o t)")
                             ).then_inc(s_a[e], 16)

            sp.wait_ge(s_sc, 2 * PEER_HEADS)
            for e in range(VG):
                v_tile(0, 0, 0, e, True)
            for n in range(4):
                sp.wait_ge(s_gst[n], 16 * (U1 + U2))
            for n in range(2):
                sp.wait_ge(s_gd[n], 16 * U2 // 2)
            for half in range(2):
                def v_round(i, first=False):
                    for r in range(2):
                        w_tiles(half, i, r, first)
                        for e in range(VG):
                            early = first and r == 0
                            a_tile(half, i, r, e, early)
                            if not early:
                                v_tile(half, i, r, e, False)
                if half == 0:
                    v_round(0, True)
                    for k in range(2):
                        sp.dma_start(cur[:, 8 * k:8 * k + 8], h_dram[:, 8 * k:8 * k + 8]).then_inc(s_hl, 16)
                with sp.Fori(1 - half, VR // 2) as i:
                    v_round(i)

        @block.gpsimd
        def _(pool):
            for q in range(4):
                pool.dma_start(cur[:, 4 * q:4 * q + 4], x_t[:, 4 * q:4 * q + 4]).then_inc(s_x[q], 16)
                if q == 0:
                    pool.dma_start(vec[:, :], vectors).then_inc(s_const, 16)
                    pool.dma_start(idn[:, :], ident).then_inc(s_const, 16)
            pool.dma_start(gup, gate_up).then_inc(s_const, 16)
            pool.dma_start(mask, scan_mask).then_inc(s_const, 16)
            with pool.Fori(0, NGLA) as h:
                for d in range(2):
                    pool.wait_ge(s_ate, 2 * h + d + 1)
                    pool.sem_inc(s_mask, 1)
                    for half in range(2):
                        a = at[64 * half:64 * half + 64, d]
                        nc.gpsimd.affine_select(
                            out=a, in_=a, compare_op=ALU.is_ge, fill=0.0, base=0,
                            pattern=[[0, NC // 2], [1 - 2 * d, CHUNK]], channel_multiplier=2 * d - 1,
                        ).then_inc(s_atm, 1)
            pool.wait_ge(s_y, 2 * NGLA)
            pool.dma_start(dist_t, dist).then_inc(s_tab, 16)
            pool.dma_start(work[:, 12:16], count).then_inc(s_tab, 16)
            pool.wait_ge(s_nlo, 2 * KD)
            for n in range(2):
                pool.dma_start(x_res[:, n], x_t[:, n]).then_inc(s_xr[n], 16)
            with pool.Fori(0, KD // 2 - 1) as i:
                for j in range(2):
                    pool.wait_ge(s_jobev, 2 * i + (JOB_OUT + j + 1))
                    pool.dma_start(x_res[:, j], x_t[:, bass.ds(2 * i + (2 + j), 1)].rearrange("p o t -> p (o t)")
                                   ).then_inc(s_xr[j], 16)
            pool.dma_start(keys, sub_keys).then_inc(s_keys, 16)
            pool.wait_ge(s_jobev, JOB_Q)
            for q in range(4):
                pool.dma_start(h_dram[:, 4 * q:4 * q + 4], cur[:, 4 * q:4 * q + 4]).then_inc(s_hsaved, 16)
            pool.wait_ge(s_hsaved, 64)
            pool.wait_ge(s_nlo, 3 * KD)
            pool.dma_start(count_up, steps).then_inc(s_keys, 16)

            def store_gelu(i, j):
                pool.wait_ge(s_jobev, 4 * i + (JOB_U + j + 1))
                pool.dma_start(gelu_dram[bass.ds(4 * i + j, 1)].rearrange("o p t -> p (o t)"), gelu_t[:, j]).then_inc(s_gst[j], 16)

            with pool.Fori(0, U1) as i:
                for j in range(4):
                    store_gelu(i, j)
            with pool.Fori(0, U2 // 2) as i:
                for r in range(2):
                    for j in range(4):
                        store_gelu(2 * i + (U1 + r), j)
                    pool.wait_ge(s_gev, 16 * i + 8 * r + 8 + BANKS_FREE)
                    pool.dma_start(gate_dram[bass.ds(2 * i + r, 1)].rearrange("o p c -> p (o c)"),
                                   gate_t[:, r].rearrange("p i t -> p (i t)")).then_inc(s_gd[r], 16)
            for q in range(4):
                pool.wait_ge(s_fin, 4 * q + 4)
                pool.dma_start(out_t.rearrange("(k p) t -> p k t", p=P)[:, 4 * q:4 * q + 4], cur[:, 4 * q:4 * q + 4]
                               ).then_inc(s_out, 16)
            pool.wait_ge(s_out, 64)

        @block.scalar
        def _(act):
            link = Chain(act, s_act)
            act.sem_inc(s_gev, BANKS_FREE)

            def split(J, first=False):
                act.wait_ge(s_raw[J.slot], 16 * (J.use + 1))
                if not first:
                    act.wait_ge(s_jobmm, J.n - 1)
                nc.scalar.copy(w_hi[:, J.slot], raw[:, J.slot]).then_inc(s_hi, 1)

            def evacuate(J, dst, rows=P):
                act.wait_ge(s_jobmm, J.n + 1)
                nc.scalar.copy(dst, psum[0:rows, J.slot]).then_inc(s_jobev, 1)

            def norm(stage, tiles, first_tile, base, ready):
                for k in range(tiles):
                    ready(k)
                    if k >= 2:
                        act.wait_ge(s_ssmm, base + k - 1)
                    nc.scalar.activation(sq_tmp[:, k % 2], cur[:, first_tile + k], ACT.Square).then_inc(s_sq, 1)
                act.wait_ge(s_rinv, stage + 1)
                nc.scalar.activation(r_t, ri_t, ACT.Sqrt).then_inc(s_r, 1)

            def halves(k, src, made):
                if made:
                    act.wait_ge(s_n, made)
                nc.scalar.copy(act_hi[:, k], src).then_inc(s_nhi, 1)

            split(job(0, 0, 0, 0), True)
            norm(0, KD, 0, 0, lambda k: act.wait_ge(s_x[k // 4], 16))
            for k in range(KD):
                halves(k, n_tmp[:, k % 2], k + 1)
            split(job(1, 0, 0, 0), True)
            evacuate(job(0, 0, 0, 0), gd, 32 + RANK)
            for j in range(GROUP):
                J = job(JOB_GROUPS, 0, 0, j)
                split(job(JOB_GROUPS + 1, 0, 0, j))
                evacuate(J, fresh[:, j])

            def next_jobs(p, first, i, groups_taken, more=True):
                if p % 3 == 0:
                    j = p // 3
                    if j:
                        evacuate(job(first, GROUP, i, j - 1), fresh[:, j - 1])
                    if j == 0:
                        act.wait_ge(s_take, groups_taken)
                    if j < GROUP and (more or j < GROUP - 1):
                        split(job(first + 1, GROUP, i, j))

            with act.Fori(0, NGLA) as h:
                link.enter(h, 4)

                def gates(d):
                    act.wait_ge(s_zb, 2 * h + d + 1)
                    link(nc.scalar.activation(ab, zb, ACT.Abs))
                    link(nc.scalar.activation(ab, ab, ACT.Exp, scale=-1.0))
                    nc.scalar.activation(ab, ab, ACT.Ln, bias=1.0).then_inc(s_ln, 1)

                def exps(d):
                    act.wait_ge(s_cum, 2 * h + d + 1)
                    b = (cum, la)[d]
                    nc.scalar.activation(zb, b, ACT.Exp, scale=1.0 / TAU).then_inc(s_e, 1)
                    nc.scalar.activation(ab, b, ACT.Exp, scale=-1.0 / TAU).then_inc(s_e, 1)
                    nc.scalar.activation(dec[:, d], cum.rearrange("p (n c) -> p n c", c=CHUNK)[:, :, CHUNK - 1],
                                         ACT.Exp, scale=1.0 / TAU).then_inc(s_dec, 1)
                    if d == 0:
                        act.wait_ge(s_exc, h + 1)
                    nc.scalar.activation(exc, exc, ACT.Exp, scale=1.0 / TAU).then_inc(s_e, 1)

                def v_rows():
                    act.wait_ge(s_vtp, h + 1)
                    for t in range(DVT):
                        nc.scalar.copy(vt[:, :, t * P:(t + 1) * P],
                                       psum[:, 5 + t].rearrange("p (a e) -> p a e", e=P)).then_inc(s_vt, 1)

                def scores(d):
                    act.wait_ge(s_att, 2 * h + d + 1)
                    nc.scalar.copy(at[:, d].rearrange("p a c -> p (a c)"), psum[:, 4, 256 * d:256 * d + 256]).then_inc(s_ate, 1)
                    act.wait_ge(s_ktp, 2 * h + d + 1)
                    nc.scalar.copy(kt[:, d], psum[:, 2 + d]).then_inc(s_kt, 1)

                def silu():
                    nc.scalar.activation(sil, taken[:, 4:6], ACT.Silu).then_inc(s_sil, 1)

                def squares():
                    for t in range(DVT):
                        act.wait_ge(s_o, 2 * h + t + 1)
                        nc.scalar.activation(osq[:, t], psum[:, 5 + t], ACT.Square).then_inc(s_osq, 1)

                def root():
                    act.wait_ge(s_ginv, h + 1)
                    nc.scalar.activation(g_r, g_ri, ACT.Sqrt).then_inc(s_gr, 1)

                at_part = {0: lambda: gates(0), 1: v_rows, 2: lambda: exps(0), 4: lambda: gates(1), 6: lambda: scores(0),
                           5: lambda: exps(1), 8: lambda: scores(1), 9: silu, 14: squares, 15: root}
                for p in range(PARTS):
                    next_jobs(p, JOB_GROUPS + GROUP, h, h + 1)
                    if p in at_part:
                        at_part[p]()
                evacuate(job(JOB_GROUPS + GROUP, GROUP, h, GROUP - 1), fresh[:, GROUP - 1])
                link.leave(NGLA)

            def attention(g, first, i, jobs, more=True):
                for p in range(PARTS):
                    if jobs:
                        next_jobs(p, first, i, NGLA + g + 1, more)
                    if p < 16:
                        act.wait_ge(s_sb, 16 * g + p + 1)
                        if p >= 2:
                            act.wait_ge(s_ptp, 16 * g + p - 1)
                        nc.scalar.activation(prob[:, p % 2], logit[:, p % 2], ACT.Exp,
                                             bias=negmax[:, p % 2:p % 2 + 1]).then_inc(s_p, 1)
                if jobs:
                    evacuate(job(first, GROUP, i, GROUP - 1), fresh[:, GROUP - 1])

            first = JOB_GROUPS + GROUP * (NGLA + 1)
            with act.Fori(0, NATT - 1) as g:
                attention(g, first, g, True)
            attention(NATT - 1, 0, 0, False)

            norm(1, 8, 8, KD, lambda k: act.wait_ge(s_ot, 2 * NATT))
            for k in range(KD):
                halves(k, cur[:, k] if k < 8 else n_tmp[:, k % 2], KD + k - 7 if k >= 8 else 0)
            with act.Fori(0, KD // 2) as i:
                for j in range(2):
                    split(job(JOB_OUT + 1, 2, i, j))
            norm(2, KD, 0, KD + 8, lambda k: act.wait_ge(s_jobev, JOB_Q))
            for k in range(KD):
                halves(k, n_tmp[:, k % 2], KD + 8 + k + 1)

            act.wait_ge(s_hsaved, 64)
            with act.Fori(0, PEER_HEADS) as i:
                for j in range(2):
                    split(job(JOB_Q + 1, 2, i, j))
                    evacuate(job(JOB_Q, 2, i, j), q_t[:, j])
                    act.wait_ge(s_scp, 2 * i + j + 1)
                    nc.scalar.copy(cur[:, :].rearrange("p (a q) t -> p a (q t)", a=TT)[:, :, bass.ds(2 * P * i + P * j, P)],
                                   psum[:, 2 + j].rearrange("p (a k) -> p a k", k=NKEYS)).then_inc(s_sc, 1)

            def gelu(J, j, stores):
                act.wait_ge(s_jobmm, J.n + 1)
                if stores is not None:
                    act.wait_ge(s_gst[j], 16 * stores)
                nc.scalar.activation(gelu_t[:, j], psum[:, J.slot], ACT.Gelu).then_inc(s_jobev, 1)

            def u1_round(i, first=False):
                for j in range(4):
                    split(job(JOB_U + 1, 4, i, j))
                    gelu(job(JOB_U, 4, i, j), j, None if first else i)
                    if j == 2:
                        for u in range(2):
                            act.wait_ge(s_tke, 2 * i + u + 1)
                            nc.scalar.activation(top_exp[:, u], top[:, u], ACT.Exp, bias=tk_neg[:, u:u + 1],
                                                 accum_out=tk_sum[:, u:u + 1]).then_inc(s_tkx, 1)

            u1_round(0, first=True)
            with act.Fori(1, U1) as i:
                u1_round(i)
            for x in range(3):
                act.wait_ge(s_rtp, x + 1)
                nc.scalar.copy(routed_t[:, x], psum[:, 2 + x]).then_inc(s_rt, 1)

            def u2_round(i, first=False, last=False):
                for r in range(2):
                    for j in range(4):
                        if not (last and r == 1 and j == 3):
                            split(job(JOB_U + 4 * U1 + 1, 8, i, 4 * r + j))
                        for q in (2 * j, 2 * j + 1):
                            act.wait_ge(s_gmm, 16 * i + 8 * r + q + 1 + HOT_FREE)
                            if q == 0 and not first:
                                act.wait_ge(s_gd[r], 16 * i)
                            nc.scalar.copy(gate_t[:, r, :, 4 * q:4 * q + 4],
                                           psum[:, 2 + q % 4].rearrange("p (t k) -> p k t", k=NKEYS)).then_inc(s_gev, 1)
                        gelu(job(JOB_U + 4 * U1, 8, i, 4 * r + j), j, 2 * i + (U1 + r))

            u2_round(0, first=True)
            with act.Fori(1, U2 // 2 - 1) as i:
                u2_round(i)
            u2_round(U2 // 2 - 1, last=True)
            act.wait_ge(s_jobmm, NJOBS)

            def v_highs(half, i, r, e, early=False):
                n = NKEYS * half + 8 * i + 4 * r + e
                act.wait_ge(s_v[e], 16 * (2 * i + (32 * half + r + 1)))
                if not early:
                    act.wait_ge(s_vmm, n - 3)
                nc.scalar.copy(v_hi[:, e], v_raw[:, e]).then_inc(s_vh, 1)
                act.wait_ge(s_w, n + 1)
                nc.scalar.copy(g_hi[:, e], weight_t[:, e % 2]).then_inc(s_wh, 1)

            for half in range(2):
                if half == 0:
                    for r in range(2):
                        for e in range(VG):
                            v_highs(0, 0, r, e, r == 0)
                with act.Fori(1 - half, VR // 2) as i:
                    for r in range(2):
                        for e in range(VG):
                            v_highs(half, i, r, e)
            norm(3, KD, 0, 2 * KD + 8, lambda k: act.wait_ge(s_vev, k + 1))

        @block.tensor
        def _(pe):
            def part(J, third, first=False):
                if third == 0:
                    pe.wait_ge(s_lo, J.n + 1)
                    if not first:
                        pe.wait_ge(s_jobev, J.n - 1)
                for k in range(CUT[third], CUT[third + 1]):
                    o = psum[:, J.slot]
                    nc.tensor.matmul(o, w_hi[:, J.slot, k], act_hi[:, k], start=(k == 0), stop=False)
                    nc.tensor.matmul(o, w_hi[:, J.slot, k], act_lo[:, k], start=False, stop=False)
                    last = nc.tensor.matmul(o, w_lo[:, J.slot, k], act_hi[:, k], start=False, stop=(k == KD - 1))
                if third == 2:
                    last.then_inc(s_jobmm, 1)

            def whole(J, first=False):
                for third in range(3):
                    part(J, third, first)

            def norm(tiles, base, bank):
                for k in range(tiles):
                    pe.wait_ge(s_sq, base + k + 1)
                    nc.tensor.matmul(psum[:, bank], ones[:, :], sq_tmp[:, k % 2], start=(k == 0),
                                     stop=(k == tiles - 1)).then_inc(s_ssmm, 1)

            pe.sem_inc(s_gmm, HOT_FREE)
            pe.wait_ge(s_ones, 1)
            norm(KD, 0, 2)
            pe.wait_ge(s_nlo, KD)
            whole(job(0, 0, 0, 0), True)
            pe.wait_ge(s_const, 64)
            for j in range(GROUP):
                whole(job(JOB_GROUPS, 0, 0, j), j == 0)

            with pe.Fori(0, NGLA) as h:
                def z():
                    pe.wait_ge(s_up, h + 1)
                    for d in range(2):
                        r = slice(32 * d, 32 * d + RANK)
                        nc.tensor.matmul(psum[:, 2 + d], up[r, :], gd[r, :], start=True, stop=True).then_inc(s_z, 1)

                def v_rows():
                    pe.wait_ge(s_take, h + 1)
                    for t in range(DVT):
                        for a in range(TT):
                            last = nc.tensor.transpose(psum[:, 5 + t, a * P:(a + 1) * P], taken[:, 2 + t, a * P:(a + 1) * P],
                                                       idn[:, :])
                    last.then_inc(s_vtp, 1)

                def scores(d):
                    pe.wait_ge(s_qk, 6 * h + 3 * d + 3)
                    if d:
                        pe.wait_ge(s_ate, 2 * h + 1)
                    for c in range(NC):
                        t = slice(CHUNK * c, CHUNK * (c + 1))
                        o = psum[64 * (c % 2):64 * (c % 2) + 64, 4, 256 * d + CHUNK * (c // 2):256 * d + CHUNK * (c // 2 + 1)]
                        last = nc.tensor.matmul(o, kd[:, d, t], qd[:, d, t], start=True, stop=True)
                    last.then_inc(s_att, 1)
                    for a in range(TT):
                        last = nc.tensor.transpose(psum[:, 2 + d, a * P:(a + 1) * P], ke[:, a * P:(a + 1) * P], idn[:, :])
                    last.then_inc(s_ktp, 1)

                def kv(n0, n1):
                    for n in range(n0, n1):
                        d, step = n % 2, n // 2
                        c = step if d == 0 else NC - 1 - step
                        if n == 0:
                            pe.wait_ge(s_kt, 2 * h + 2)
                            pe.wait_ge(s_ate, 2 * h + 2)
                            pe.wait_ge(s_vt, 2 * h + 2)
                        if n >= 4:
                            pe.wait_ge(s_st, 14 * h + n - 3)
                        r = slice(64 * (c % 2), 64 * (c % 2) + 64)
                        nc.tensor.matmul(psum[:, KV_BANKS[n % 4], 0:DV],
                                         kt[r, d, (c // 2) * P:(c // 2 + 1) * P], vt[r, c // 2, :],
                                         start=True, stop=True).then_inc(s_kv, 1)

                def outputs():
                    pe.wait_ge(s_ats, 2 * h + 2)
                    pe.wait_ge(s_st, 14 * h + 14)
                    for t in range(DVT):
                        for a in range(NC // 2):
                            pair = slice(P * a, P * (a + 1))
                            nc.tensor.matmul(psum[:, 5 + t, pair], vt[:, a, t * P:(t + 1) * P], at_sum[:, a, :],
                                             start=True, stop=False)
                            for c in (2 * a, 2 * a + 1):
                                for d in range(2):
                                    if (c, d) in ((0, 0), (NC - 1, 1)):
                                        continue
                                    cols = slice(CHUNK * c, CHUNK * (c + 1))
                                    last = nc.tensor.matmul(
                                        psum[:, 5 + t, cols], state[:, c, DV * d + t * P:DV * d + (t + 1) * P], qd[:, d, cols],
                                        start=False, stop=(c % 2 == 1 and (d == 1 or c == NC - 1)))
                        last.then_inc(s_o, 1)

                def mean_square():
                    for t in range(DVT):
                        pe.wait_ge(s_osq, 2 * h + t + 1)
                        last = nc.tensor.matmul(psum[:, 2], ones[:, :], osq[:, t], start=(t == 0), stop=(t == DVT - 1))
                    last.then_inc(s_oss, 1)

                at_part = {0: z, 1: v_rows, 5: lambda: scores(0), 7: lambda: scores(1), 8: lambda: kv(0, 4),
                           9: lambda: kv(4, 8), 10: lambda: kv(8, 12), 11: lambda: kv(12, 14), 13: outputs, 14: mean_square}
                for p in range(PARTS):
                    part(job(JOB_GROUPS + GROUP, GROUP, h, p // 3), p % 3)
                    if p in at_part:
                        at_part[p]()

            def attention(g, first, i, jobs):
                def v_rows(pr):
                    if pr == 0:
                        pe.wait_ge(s_take, NGLA + g + 1)
                    for a in range(TT):
                        last = nc.tensor.transpose(psum[:, 7 - pr, a * P:(a + 1) * P], taken[:, 3 * pr + 2, a * P:(a + 1) * P],
                                                   idn[:, :])
                    last.then_inc(s_avp, 1)

                def out_rows(pr):
                    pe.wait_ge(s_nrm, 16 * g + 8 * pr + 8)
                    if pr == 0:
                        pe.wait_ge(s_av, 2 * g + 1)
                    else:
                        pe.wait_ge(s_ot, 2 * g + 1)
                    for a in range(TT):
                        last = nc.tensor.transpose(psum[:, 7, a * P:(a + 1) * P], att_rows[:, a, :], idn[:, :])
                    last.then_inc(s_otp, 1)

                for p in range(PARTS):
                    if jobs:
                        part(job(first, GROUP, i, p // 3), p % 3)
                    if p == 0:
                        v_rows(0)
                        v_rows(1)
                    if p < 16:
                        pr, hd, a = p // 8, (p // 4) % 2, p % 4
                        r = slice(HD * hd, HD * hd + HD)
                        nc.tensor.matmul(psum[:, 2 + p % 2], taken[r, 3 * pr, a * P:(a + 1) * P], taken[r, 3 * pr + 1, :],
                                         start=True, stop=True).then_inc(s_qkm, 1)
                    if 1 <= p <= 16:
                        u = p - 1
                        pe.wait_ge(s_p, 16 * g + u + 1)
                        if u >= 2:
                            pe.wait_ge(s_pt, 16 * g + u - 1)
                        for s in range(TT):
                            last = nc.tensor.transpose(psum[:, 4 + u % 2, s * P:(s + 1) * P], prob[:, u % 2, s * P:(s + 1) * P],
                                                       idn[:, :])
                        last.then_inc(s_ptp, 1)
                    if p == 10:
                        out_rows(0)
                    if p >= 2:
                        u = p - 2
                        pr, hd = u // 8, (u // 4) % 2
                        pe.wait_ge(s_pt, 16 * g + u + 1)
                        if u == 0:
                            pe.wait_ge(s_av, 2 * g + 2)
                        if u >= 1:
                            pe.wait_ge(s_nrm, 16 * g + u)
                        for s in range(TT):
                            last = nc.tensor.matmul(psum[:, 6, (u % 2) * P:(u % 2) * P + HD + 1],
                                                    prob_t[:, u % 2, s * P:(s + 1) * P], va[:, pr, s, hd, :],
                                                    start=(s == 0), stop=(s == TT - 1))
                        last.then_inc(s_pv, 1)
                out_rows(1)

            first = JOB_GROUPS + GROUP * (NGLA + 1)
            with pe.Fori(0, NATT - 1) as g:
                attention(g, first, g, True)
            attention(NATT - 1, 0, 0, False)

            norm(8, KD, 2)
            pe.wait_ge(s_nlo, 2 * KD)
            with pe.Fori(0, KD // 2) as i:
                for j in range(2):
                    whole(job(JOB_OUT, 2, i, j))
            norm(KD, KD + 8, 2)

            def key_scores(i, j):
                pe.wait_ge(s_jobev, 2 * i + (JOB_Q + j + 1))
                for a in range(TT):
                    last = nc.tensor.matmul(psum[:, 2 + j, a * P:(a + 1) * P], q_t[:, j, a * P:(a + 1) * P],
                                            keys[:, bass.ds(2 * i + j, 1)].rearrange("p o k -> p (o k)"), start=True, stop=True)
                last.then_inc(s_scp, 1)

            pe.wait_ge(s_nlo, 3 * KD)
            pe.wait_ge(s_keys, 32)
            with pe.Fori(0, PEER_HEADS) as i:
                whole(job(JOB_Q, 2, i, 0))
                part(job(JOB_Q, 2, i, 1), 0)
                key_scores(i, 0)
                part(job(JOB_Q, 2, i, 1), 1)
                part(job(JOB_Q, 2, i, 1), 2)
                key_scores(i, 1)
            with pe.Fori(0, U1) as i:
                for j in range(4):
                    whole(job(JOB_U, 4, i, j))
            pe.wait_ge(s_route, 6 * U1)
            pe.wait_ge(s_sc, 2 * PEER_HEADS)
            for x in range(3):
                for a in range(TT):
                    last = nc.tensor.transpose(psum[:, 2 + x, a * P:(a + 1) * P], routed[:, x, a * P:(a + 1) * P], idn[:, :])
                last.then_inc(s_rtp, 1)

            def outer(i, r, q):
                n = 16 * i + 8 * r + q
                pe.wait_ge(s_hot, n + 1)
                if r == 0 and q < 4:
                    pe.wait_ge(s_rt, 3)
                pe.wait_ge(s_gev, n - 3 + BANKS_FREE)
                for t in range(4):
                    o = psum[:, 2 + q % 4, t * P:(t + 1) * P]
                    last = nc.tensor.matmul(o, hot2[:, 4 * (q % 2) + t], hot1[:, 4 * (q % 2) + t], start=True, stop=True)
                last.then_inc(s_gmm, 1)

            with pe.Fori(0, U2 // 2) as i:
                for r in range(2):
                    for j in range(4):
                        J = job(JOB_U + 4 * U1, 8, i, 4 * r + j)
                        part(J, 0)
                        outer(i, r, 2 * j)
                        part(J, 1)
                        outer(i, r, 2 * j + 1)
                        part(J, 2)

            zero = at_sum[:, :, :].rearrange("p a c -> p (a c)")

            def v_products(half, i, r, e):
                n = NKEYS * half + 8 * i + 4 * r + e
                pe.wait_ge(s_vl, n + 1)
                pe.wait_ge(s_wl, n + 1)
                for m in range(HT):
                    c = slice(P * m, P * (m + 1))
                    nc.tensor.matmul(psum[:, m], v_hi[:, e, c], g_hi[:, e], start=False, stop=False)
                    nc.tensor.matmul(psum[:, m], v_hi[:, e, c], g_lo[:, e], start=False, stop=False)
                    last = nc.tensor.matmul(psum[:, m], v_lo[:, e, c], g_hi[:, e], start=False, stop=False)
                last.then_inc(s_vmm, 1)

            pe.wait_ge(s_jobev, NJOBS)
            pe.wait_ge(s_gev, 8 * U2 + BANKS_FREE)
            for half in range(2):
                for m in range(HT):
                    if half:
                        pe.wait_ge(s_vev, m + 1)
                    nc.tensor.matmul(psum[:, m], zero[:, 0:P], zero, start=True, stop=False)
                with pe.Fori(0, VR // 2) as i:
                    for r in range(2):
                        for e in range(VG):
                            v_products(half, i, r, e)
                for m in range(HT):
                    nc.tensor.matmul(psum[:, m], zero[:, 0:P], zero, start=False, stop=True).then_inc(s_vend, 1)
            pe.wait_ge(s_vev, HT + 3)
            norm(KD, 2 * KD + 8, 2)

        @block.vector
        def _(vec_e):
            dve = vec_e
            link = Chain(dve, s_vec)

            def rest(J):
                dve.wait_ge(s_hi, J.n + 1)
                nc.vector.tensor_tensor(w_lo[:, J.slot], raw[:, J.slot], w_hi[:, J.slot].bitcast(F32), ALU.subtract
                                        ).then_inc(s_lo, 1)

            def inverse(ms, width, dst, done):
                link(nc.vector.tensor_scalar(dst, ms, 1.0 / width, EPS, ALU.mult, ALU.add))
                nc.vector.reciprocal(dst, dst).then_inc(done, 1)

            def norm(stage, base, tiles, width, col, n_base, plain=0):
                dve.wait_ge(s_ssmm, base + tiles)
                inverse(psum[:, 2], width, ri_t, s_rinv)
                dve.wait_ge(s_r, stage + 1)

                def low(k):
                    dve.wait_ge(s_nhi, stage * KD + k + 1)
                    src = cur[:, k] if k < plain else n_tmp[:, k % 2]
                    nc.vector.tensor_tensor(act_lo[:, k], src, act_hi[:, k].bitcast(F32), ALU.subtract).then_inc(s_nlo, 1)

                for k in range(KD):
                    if k >= plain:
                        if k > 1:
                            dve.wait_ge(s_nlo, stage * KD + k - 1)
                        nc.vector.scalar_tensor_tensor(out=n_tmp[:, k % 2], in0=cur[:, k], scalar=vec[:, col + k - plain:col + k - plain + 1],
                                                       in1=r_t, op0=ALU.mult, op1=ALU.mult).then_inc(s_n, 1)
                        dve.wait_ge(s_n, n_base + k - plain + 1)
                    if k:
                        low(k - 1)
                low(KD - 1)

            nc.vector.memset(ones[:, :], 1.0).then_inc(s_ones, 1)
            link(nc.vector.memset(at_sum[:, :, :], 0.0))
            rest(job(0, 0, 0, 0))
            dve.wait_ge(s_const, 64)
            norm(0, 0, KD, D, V_N1, 0)
            rest(job(1, 0, 0, 0))
            for j in range(GROUP):
                rest(job(JOB_GROUPS + 1, 0, 0, j))

            with dve.Fori(0, NGLA) as h:
                link.enter(h, VEC_GLA)

                def take():
                    dve.wait_ge(s_jobev, JOB_GROUPS + GROUP * (h + 1))
                    nc.vector.tensor_copy(taken, fresh).then_inc(s_take, 1)
                    dve.wait_ge(s_take, h + 1)
                    link(nc.vector.tensor_copy(bias, vec[:, bass.ds(h * 2 + V_BIAS, 2)]))
                    nc.vector.tensor_copy(up[:, :], gup[:, bass.ds(h * DK, DK)]).then_inc(s_up, 1)

                def gate_in(d):
                    dve.wait_ge(s_z, 2 * h + d + 1)
                    if d:
                        dve.wait_ge(s_qk, 6 * h + 3)
                    nc.vector.tensor_scalar(zb, psum[:, 2 + d], bias[:, d:d + 1], None, ALU.add).then_inc(s_zb, 1)

                def cumulate(d):
                    dve.wait_ge(s_ln, 2 * h + d + 1)
                    link(nc.vector.scalar_tensor_tensor(out=la, in0=zb, scalar=0.0, in1=ab, op0=ALU.min, op1=ALU.subtract))
                    scan = nc.vector.tensor_tensor_scan(cum, mask, la, 0.0, ALU.mult, ALU.add)
                    cum_c = cum.rearrange("p (n c) -> p n c", c=CHUNK)
                    exc_c, la_c = exc.rearrange("p (n c) -> p n c", c=CHUNK), la.rearrange("p (n c) -> p n c", c=CHUNK)
                    total = cum_c[:, :, CHUNK - 1:CHUNK].broadcast_to([P, NC, CHUNK])
                    if d == 0:
                        scan.then_inc(s_cum, 1)
                        dve.wait_ge(s_cum, 2 * h + 1)
                        nc.vector.tensor_tensor(exc_c, total, cum_c, ALU.subtract).then_inc(s_exc, 1)
                    else:
                        link(scan)
                        link(nc.vector.tensor_tensor(exc, cum, la, ALU.subtract))
                        nc.vector.tensor_tensor(la_c, total, exc_c, ALU.subtract).then_inc(s_cum, 1)

                def decayed(d):
                    dve.wait_ge(s_e, 6 * h + 3 * d + 1)
                    nc.vector.scalar_tensor_tensor(out=qd[:, d], in0=taken[:, 0], scalar=float(DK) ** -0.5, in1=zb,
                                                   op0=ALU.mult, op1=ALU.mult).then_inc(s_qk, 1)
                    dve.wait_ge(s_e, 6 * h + 3 * d + 2)
                    nc.vector.tensor_tensor(kd[:, d], taken[:, 1], ab, ALU.mult).then_inc(s_qk, 1)
                    dve.wait_ge(s_e, 6 * h + 3 * d + 3)
                    if d:
                        dve.wait_ge(s_ktp, 2 * h + 1)
                    nc.vector.tensor_tensor(ke, taken[:, 1], exc, ALU.mult).then_inc(s_qk, 1)

                def states(n0, n1):
                    for n in range(n0, n1):
                        d, step = n % 2, n // 2
                        c = step if d == 0 else NC - 1 - step
                        to = c + 1 if d == 0 else c - 1
                        dve.wait_ge(s_kv, 14 * h + n + 1)
                        new, got = state[:, to, DV * d:DV * (d + 1)], psum[:, KV_BANKS[n % 4], 0:DV]
                        if step == 0:
                            if n == 0:
                                dve.wait_ge(s_dec, 2 * h + 2)
                            nc.vector.tensor_copy(new, got).then_inc(s_st, 1)
                        else:
                            dve.wait_ge(s_st, 14 * h + n - 1)
                            nc.vector.scalar_tensor_tensor(out=new, in0=state[:, c, DV * d:DV * (d + 1)],
                                                           scalar=dec[:, d, c:c + 1], in1=got, op0=ALU.mult,
                                                           op1=ALU.add).then_inc(s_st, 1)

                def add_scores():
                    dve.wait_ge(s_atm, 4 * h + 4)
                    for half in range(2):
                        r = slice(64 * half, 64 * half + 64)
                        nc.vector.tensor_tensor(at_sum[r, :, CHUNK * half:CHUNK * (half + 1)], at[r, 0], at[r, 1], ALU.add
                                                ).then_inc(s_ats, 1)

                def gate_rms():
                    dve.wait_ge(s_oss, h + 1)
                    inverse(psum[:, 2], DV, g_ri, s_ginv)

                def gated():
                    dve.wait_ge(s_gr, h + 1)
                    dve.wait_ge(s_sil, h + 1)
                    for t in range(DVT):
                        link(nc.vector.scalar_tensor_tensor(out=osq[:, t], in0=psum[:, 5 + t], scalar=vec[:, V_GLA + t:V_GLA + t + 1],
                                                            in1=g_r, op0=ALU.mult, op1=ALU.mult))
                        nc.vector.tensor_tensor(cur[:, bass.ds(2 * h + t, 1)].rearrange("p o t -> p (o t)"), osq[:, t], sil[:, t],
                                                ALU.mult).then_inc(s_y, 1)

                at_part = {0: lambda: (take(), gate_in(0)), 2: lambda: (cumulate(0), decayed(0)), 4: lambda: gate_in(1),
                           5: lambda: (cumulate(1), decayed(1)),
                           8: lambda: states(0, 4), 9: lambda: states(4, 8), 10: lambda: (add_scores(), states(8, 12)),
                           11: lambda: states(12, 14), 15: gate_rms, 16: gated}
                for p in range(PARTS):
                    if p == 0:
                        at_part[p]()
                    if p % 3 == 0:
                        rest(job(JOB_GROUPS + GROUP + 1, GROUP, h, p // 3))
                    if p in at_part and p:
                        at_part[p]()
                dve.wait_ge(s_y, 2 * h + 2)
                link.leave(NGLA)

            def attention(g, first, i, jobs):
                def take():
                    dve.wait_ge(s_jobev, GROUP * (NGLA + g + 1) + JOB_GROUPS)
                    q_in, q_out = fresh.rearrange("p (r j) t -> p r j t", j=3), taken.rearrange("p (r j) t -> p r j t", j=3)
                    link(nc.vector.tensor_scalar(q_out[:, :, 0], q_in[:, :, 0], float(HD) ** -0.5, None, ALU.mult))
                    nc.vector.tensor_copy(q_out[:, :, 1:3], q_in[:, :, 1:3]).then_inc(s_take, 1)
                    link(nc.vector.tensor_copy(slope, vec[:, bass.ds(g * 4 + V_SLOPE, 4)]))
                    for pr in range(2):
                        dve.wait_ge(s_avp, 2 * g + pr + 1)
                        nc.vector.tensor_copy(va[:, pr, :, :, 0:HD], psum[:, 7 - pr].rearrange("p (s h e) -> p s h e", h=2, e=HD)
                                              ).then_inc(s_av, 1)

                def out_tile(pr):
                    dve.wait_ge(s_otp, 2 * g + pr + 1)
                    nc.vector.tensor_copy(cur[:, bass.ds(2 * g + (8 + pr), 1)].rearrange("p o t -> p (o t)"), psum[:, 7]
                                          ).then_inc(s_ot, 1)

                for p in range(PARTS):
                    if p == 0:
                        take()
                    if jobs and p % 3 == 0:
                        rest(job(first + 1, GROUP, i, p // 3))
                    if p < 16:
                        hd, a = p // 4, p % 4
                        dve.wait_ge(s_qkm, 16 * g + p + 1)
                        if p >= 2:
                            dve.wait_ge(s_p, 16 * g + p - 1)
                            dve.wait_ge(s_sb, 16 * g + p - 1)
                        link(nc.vector.scalar_tensor_tensor(out=logit[:, p % 2], in0=dist_t[:, a], scalar=slope[:, hd:hd + 1],
                                                            in1=psum[:, 2 + p % 2], op0=ALU.mult, op1=ALU.add))
                        nc.vector.tensor_reduce(negmax[:, p % 2:p % 2 + 1], logit[:, p % 2], AX.X, ALU.max, negate=True
                                                ).then_inc(s_sb, 1)
                    if 1 <= p <= 16:
                        u = p - 1
                        dve.wait_ge(s_ptp, 16 * g + u + 1)
                        if u >= 2:
                            dve.wait_ge(s_pv, 16 * g + u - 1)
                        nc.vector.tensor_tensor(prob_t[:, u % 2].rearrange("p (s t) -> p s t", t=P),
                                                psum[:, 4 + u % 2].rearrange("p (s t) -> p s t", t=P),
                                                count_t[:, :, (u % 4) * P:(u % 4 + 1) * P], ALU.mult).then_inc(s_pt, 1)
                    if p == 10:
                        out_tile(0)
                    if p >= 2:
                        u = p - 2
                        hd = (u // 4) % 2
                        dve.wait_ge(s_pv, 16 * g + u + 1)
                        if u:
                            dve.wait_ge(s_nrm, 16 * g + u)
                        o = psum[:, 6, (u % 2) * P:(u % 2) * P + HD + 1]
                        link(nc.vector.reciprocal(rden, o[:, HD:HD + 1]))
                        nc.vector.tensor_scalar(att_rows[:, u % 4, HD * hd:HD * (hd + 1)], o[:, 0:HD], rden, None, ALU.mult
                                                ).then_inc(s_nrm, 1)
                dve.wait_ge(s_nrm, 16 * g + 16)
                out_tile(1)

            dve.wait_ge(s_tab, 32)
            link(nc.vector.tensor_copy(count_t, work[:, 12:16]))
            link(nc.vector.memset(va[:, :, :, :, HD:HD + 1], 1.0))
            first = JOB_GROUPS + GROUP * (NGLA + 1)
            with dve.Fori(0, NATT - 1) as g:
                link.enter(g, VEC_ATT)
                attention(g, first, g, True)
                link.leave(NATT - 1)
            attention(NATT - 1, 0, 0, False)

            norm(1, KD, 8, 8 * P, V_ATT, KD, plain=8)
            with dve.Fori(0, KD // 2) as i:
                for j in range(2):
                    J = job(JOB_OUT, 2, i, j)
                    rest(job(JOB_OUT + 1, 2, i, j))
                    dve.wait_ge(s_jobmm, J.n + 1)
                    dve.wait_ge(s_xr[j], 16 * i + 16)
                    nc.vector.tensor_tensor(cur[:, bass.ds(2 * i + j, 1)].rearrange("p o t -> p (o t)"), psum[:, J.slot],
                                            x_res[:, j], ALU.add).then_inc(s_jobev, 1)
            norm(2, KD + 8, KD, D, V_N2, KD + 8)
            link(nc.vector.memset(at_sum[:, :, :], 0.0))
            with dve.Fori(0, PEER_HEADS) as i:
                for j in range(2):
                    rest(job(JOB_Q + 1, 2, i, j))

            def apart():
                dve.sem_inc(s_apart, 1)

            def sixteen(values, cut, best, where):
                apart()
                link(nc.vector.max(best[:, 0:8], values))
                apart()
                link(nc.vector.max_index(where[:, 0:8], best[:, 0:8], values))
                apart()
                link(nc.vector.match_replace(cut, best[:, 0:8], values, LOW))
                apart()
                link(nc.vector.max(best[:, 8:16], cut))
                apart()
                link(nc.vector.max_index(where[:, 8:16], best[:, 8:16], cut))

            def top_pairs(i, u):
                link(nc.vector.tensor_copy(tk_in.rearrange("p c k -> p (c k)"), score_t[:, bass.ds(512 * i + 256 * u, 256)]))
                for c in range(2):
                    sixteen(tk_in[:, c], tk_cut[:, c], val[:, c], idx[:, c])
                sums = pair_sum.rearrange("p (a b) -> p a b", b=TOPK)
                link(nc.vector.tensor_tensor(sums, val[:, 0].unsqueeze(2).broadcast_to([P, TOPK, TOPK]),
                                             val[:, 1].unsqueeze(1).broadcast_to([P, TOPK, TOPK]), ALU.add))
                sixteen(pair_sum, pair_cut, top[:, u], place)
                nc.vector.tensor_scalar(tk_neg[:, u:u + 1], top[:, u, 0:1], -1.0, None, ALU.mult).then_inc(s_tke, 1)
                link(nc.vector.tensor_single_scalar(place_2[:, 0], place, 4, ALU.logical_shift_right))
                link(nc.vector.tensor_single_scalar(place_2[:, 1], place, TOPK - 1, ALU.bitwise_and))
                link(nc.vector.tensor_copy(place_f, place_2))
                link(nc.vector.tensor_copy(idx_f, idx))
                for c in range(2):
                    link(nc.vector.tensor_tensor(picked, place_f[:, c].unsqueeze(2).broadcast_to([P, TOPK, TOPK]),
                                                 count_up[:, 0:TOPK].unsqueeze(1).broadcast_to([P, TOPK, TOPK]), ALU.is_equal))
                    link(nc.vector.tensor_tensor(chosen, picked, idx_f[:, c].unsqueeze(1).broadcast_to([P, TOPK, TOPK]), ALU.mult))
                    nc.vector.tensor_reduce(routed[:, 1 + c, bass.ds(32 * i + 16 * u, TOPK)], chosen, AX.X, ALU.add
                                            ).then_inc(s_route, 1)
                    dve.wait_ge(s_route, 6 * i + 2 * u + c + 1)

            def gates_of(i):
                for u in range(2):
                    dve.wait_ge(s_tkx, 2 * i + u + 1)
                    link(nc.vector.reciprocal(tk_inv[:, u:u + 1], tk_sum[:, u:u + 1]))
                    nc.vector.tensor_scalar(routed[:, 0, bass.ds(32 * i + 16 * u, TOPK)], top_exp[:, u], tk_inv[:, u:u + 1], None,
                                            ALU.mult).then_inc(s_route, 1)

            dve.wait_ge(s_sc, 2 * PEER_HEADS)
            dve.wait_ge(s_keys, 32)
            with dve.Fori(0, U1) as i:
                link.enter(i, VEC_TOP)
                for j in range(4):
                    rest(job(JOB_U + 1, 4, i, j))
                    if j < 2:
                        top_pairs(i, j)
                gates_of(i)
                dve.wait_ge(s_route, 6 * i + 6)
                link.leave(U1)

            def hot(i, r, q):
                n = 16 * i + 8 * r + q
                dve.wait_ge(s_gmm, n - 1 + HOT_FREE)
                for t in range(4):
                    col = slice(4 * q + t, 4 * q + t + 1)
                    nc.vector.tensor_scalar(hot2[:, 4 * (q % 2) + t], count_up, route_tb[:, r, 2, col], None, ALU.is_equal)
                    last = nc.vector.tensor_scalar(hot1[:, 4 * (q % 2) + t], count_up, route_tb[:, r, 1, col],
                                                   route_tb[:, r, 0, col], ALU.is_equal, ALU.mult)
                last.then_inc(s_hot, 1)

            dve.wait_ge(s_rt, 3)

            def u2_round(i, last=False):
                for r in range(2):
                    link(nc.vector.tensor_copy(route_tb[:, r], routed_t[:, :, bass.ds(2 * TB * i + TB * r, TB)]))
                    for j in range(4):
                        if not (last and r == 1 and j == 3):
                            rest(job(JOB_U + 4 * U1 + 1, 8, i, 4 * r + j))
                        hot(i, r, 2 * j)
                        hot(i, r, 2 * j + 1)
                    dve.wait_ge(s_hot, 16 * i + 8 * r + 8)

            with dve.Fori(0, U2 // 2 - 1) as i:
                link.enter(i, 2)
                u2_round(i)
                link.leave(U2 // 2 - 1)
            u2_round(U2 // 2 - 1, last=True)

            def v_rest(half, i, r, e, early=False):
                n = NKEYS * half + 8 * i + 4 * r + e
                if e == 0:
                    dve.wait_ge(s_g[r], 16 * (i + (16 * half + 1)))
                dve.wait_ge(s_a[e], 16 * (2 * i + (32 * half + r + 1)))
                if not (early and r == 0 and e < 2):
                    dve.wait_ge(s_wh, n - 1)
                    dve.wait_ge(s_wl, n - 1)
                nc.vector.tensor_tensor(weight_t[:, e % 2].rearrange("p (b t) -> p b t", t=TB), g_t[:, r, :, e],
                                        a_t[:, e].rearrange("p (b t) -> p b t", t=TB), ALU.mult).then_inc(s_w, 1)
                dve.wait_ge(s_vh, n + 1)
                nc.vector.tensor_tensor(v_lo[:, e], v_raw[:, e], v_hi[:, e].bitcast(F32), ALU.subtract).then_inc(s_vl, 1)
                dve.wait_ge(s_wh, n + 1)
                nc.vector.tensor_tensor(g_lo[:, e], weight_t[:, e % 2], g_hi[:, e].bitcast(F32), ALU.subtract).then_inc(s_wl, 1)

            for half in range(2):
                if half == 0:
                    for r in range(2):
                        for e in range(VG):
                            v_rest(0, 0, r, e, True)
                with dve.Fori(1 - half, VR // 2) as i:
                    for r in range(2):
                        for e in range(VG):
                            v_rest(half, i, r, e)
                dve.wait_ge(s_hl, 32)
                for m in range(HT):
                    dve.wait_ge(s_vend, HT * half + m + 1)
                    nc.vector.tensor_tensor(cur[:, HT * half + m], cur[:, HT * half + m], psum[:, m], ALU.add).then_inc(s_vev, 1)

            dve.wait_ge(s_ssmm, 3 * KD + 8)
            inverse(psum[:, 2], D, ri_t, s_rinv)
            dve.wait_ge(s_r, 4)
            for k in range(KD):
                nc.vector.scalar_tensor_tensor(out=cur[:, k], in0=cur[:, k], scalar=vec[:, V_NF + k:V_NF + k + 1], in1=r_t,
                                               op0=ALU.mult, op1=ALU.mult).then_inc(s_fin, 1)


def weight_tiles(w):
    n = w.shape[1] // P
    return w.reshape(KD, P, n, P).transpose(2, 1, 0, 3).reshape(n, P, KD * P)


def constants():
    t = np.arange(T)
    gap = np.abs(t[:, None] - t[None, :])
    reached = [(gap % r == 0) & (gap <= w // 2) for w, r in PATTERNS]
    count = sum(x.astype(np.float32) for x in reached)
    dist = np.where(count > 0, -gap, NEG).astype(np.float32)
    tiles = lambda a: np.ascontiguousarray(a.reshape(TT, P, T).transpose(1, 0, 2))
    mask = np.tile((t % CHUNK != 0).astype(np.float32), (P, 1))
    steps = np.tile(np.arange(P, dtype=np.float32), (P, 1))
    return tiles(dist), tiles(count), np.eye(P, dtype=np.float32), mask, steps


def layout(a):
    w_in = a["w_in"][0]
    qk, vg, att = GLA_HEADS * DK, GLA_HEADS * DV, ATT_HEADS * HD
    at = np.cumsum([0, qk, qk, vg, vg, RANK, RANK, att, att, att])
    gq, gk, gv, gr, gf, gb, aq, ak, av = [w_in[:, at[n]:at[n + 1]] for n in range(9)]
    gate = np.zeros((D, P), np.float32)
    gate[:, 0:RANK], gate[:, 32:32 + RANK] = gf, gb
    cols = [gate]
    for h in range(GLA_HEADS):
        k, v = slice(DK * h, DK * (h + 1)), slice(DV * h, DV * (h + 1))
        cols += [gq[:, k], gk[:, k], gv[:, v], gr[:, v]]
    for h in range(ATT_HEADS // 2):
        c = slice(P * h, P * (h + 1))
        cols += [aq[:, c], ak[:, c], av[:, c]]
    cols += [a["w_out"][0], a["peer_w_q"][0], a["peer_u"][0].T]
    weights = np.concatenate([weight_tiles(np.concatenate(cols[:1 + 4 * GLA_HEADS + 3 * ATT_HEADS // 2], axis=1))]
                             + [weight_tiles(c) for c in cols[-3:]])
    col = lambda v: v.reshape(-1, P).T
    bias = np.stack([a["gla_gate_bias_f"][0].reshape(GLA_HEADS, DK), a["gla_gate_bias_b"][0].reshape(GLA_HEADS, DK)], 1)
    slopes = np.tile((2.0 ** (-8.0 * np.arange(1, ATT_HEADS + 1) / ATT_HEADS)).astype(np.float32), (P, 1))
    vectors = np.concatenate([col(a["norm1_g"][0]), col(a["norm2_g"][0]), col(a["final_norm_g"]), col(a["att_norm_g"][0]),
                              col(a["gla_norm_g"][0]), bias.reshape(-1, P).T, slopes], axis=1)
    gate_up = np.zeros((32 + RANK, qk), np.float32)
    gate_up[0:RANK], gate_up[32:] = a["gla_gate_up_f"][0], a["gla_gate_up_b"][0]
    dist, count, ident, mask, steps = constants()
    return {
        "x_t": np.ascontiguousarray(a["x"][0].T.reshape(KD, P, T).transpose(1, 0, 2)),
        "weights": weights,
        "peer_v": a["peer_v"][0],
        "sub_keys": np.ascontiguousarray(a["peer_sub_keys"][0].reshape(2 * PEER_HEADS, NKEYS, P).transpose(2, 0, 1)),
        "vectors": np.ascontiguousarray(vectors), "gate_up": gate_up,
        "dist": dist, "count": count, "ident": ident, "scan_mask": mask, "steps": steps,
    }


def kernel(**inputs):
    import concourse.bacc as bacc
    from concourse.bass_utils import run_bass_kernel_spmd

    nc = bacc.Bacc("TRN2", target_bir_lowering=False, num_devices=1)
    arrays = layout({k: np.asarray(v) for k, v in inputs.items()})
    args = [nc.dram_tensor(n, a.shape, mybir.dt.from_np(a.dtype), kind="ExternalInput").ap() for n, a in arrays.items()]
    out_t = nc.dram_tensor("out_t", (D, T), F32, kind="ExternalOutput").ap()
    layer(nc, *args, out_t)
    r = run_bass_kernel_spmd(nc, [arrays], core_ids=[0])
    return np.ascontiguousarray(r.results[0]["out_t"].T).reshape(1, T, D)
```

```python
from collections import namedtuple
from contextlib import ExitStack

import concourse.bass as bass
import numpy as np
from concourse import mybir

F32 = mybir.dt.float32
U8 = mybir.dt.uint8
F32R = mybir.dt.float32r
U32 = mybir.dt.uint32
ALU = mybir.AluOpType
ACT = mybir.ActivationFunctionType
AX = mybir.AxisListType

P = 128
T = 512
TT = T // P
D = 2048
KD = D // P
GLA_HEADS, DK, DV, RANK, CHUNK = 4, 128, 256, 16, 64
NC = T // CHUNK
DVT = DV // P
ATT_HEADS, HD = 16, 64
NKEYS, PEER_HEADS, TOPK = 128, 8, 16
EPS = 1e-6
TAU = 16.0
PATTERNS = ((128, 1), (512, 4), (2048, 16))
NEG = -1e30
LOW = -3.0e38

JOB_GATE = 0
GROUP = 6
NGLA = GLA_HEADS
NATT = ATT_HEADS // 4
JOB_GROUPS = 1
JOB_OUT = JOB_GROUPS + GROUP * (NGLA + NATT)
HK = KD // 2
NPAIR = 7
JOB_WHOLE = JOB_OUT + NPAIR
JOB_ATT = JOB_WHOLE + 2
JOB_Q = JOB_OUT + KD
JOB_U = JOB_Q + 2 * PEER_HEADS
NJOBS = JOB_U + NKEYS
SQ_BASE = (0, KD, KD + 8, 2 * KD + 8)
Y_SQUARES, Y_HALVES = (2, 3, 4, 5, 6, 7, 13), (0, 0, 0, 0, 1, 1, 1, 1)
PAIR_PART = 2
PARTS = 3 * GROUP
CUT = (0, 6, 11, KD)

V_N1, V_N2, V_NF, V_ATT, V_GLA, V_BIAS, V_SLOPE = 0, KD, 2 * KD, 3 * KD, 3 * KD + 8, 3 * KD + 10, 3 * KD + 18
NVEC = V_SLOPE + ATT_HEADS

VEC_TOP = 52
BANKS_FREE, HOT_FREE = 4, 2
KV_BANKS = (2, 3, 4, 7)
VEC_GLA, VEC_ATT = 8, 34
U1 = 16
U2 = 16
TB = T // U2
VG = 4
VR = NKEYS // VG
HALF = D // 2
HT = HALF // P

Job = namedtuple("Job", "n slot use")


def job(first, per, i, j):
    slot = (first + j) % 2
    return Job(first + per * i + j, slot, (first + j - slot) // 2 + (per // 2) * i)


class Chain:

    def __init__(self, eng, sem):
        self.eng, self.sem, self.n, self.base = eng, sem, 0, 0

    def __call__(self, ins):
        self.n += 1
        ins.then_inc(self.sem, 1)
        self.eng.wait_ge(self.sem, self.base + self.n)

    def enter(self, i, per):
        self.outer, self.per = (self.base, self.n), per
        self.base, self.n = self.base + self.n + i * per, 0

    def leave(self, rounds):
        assert self.n == self.per, (self.n, self.per)
        self.base, self.n = self.outer[0], self.outer[1] + rounds * self.per


def layer(nc, x_t, weights, peer_v, sub_keys, vectors, gate_up, dist, count, ident, scan_mask, steps, out_t):
    with ExitStack() as ctx:
        def sb(name, shape, dt=F32):
            return ctx.enter_context(nc.sbuf_tensor(name, shape, dt))

        def sem(name):
            return ctx.enter_context(nc.semaphore(name))

        psum = ctx.enter_context(nc.psum_tensor("psum", [P, 8, T], F32))
        act_hi, act_lo = sb("act_hi", [P, KD, T], F32R), sb("act_lo", [P, KD, T], F32R)
        raw = sb("raw", [P, 2, KD, P])
        w_hi, w_lo = sb("w_hi", [P, 2, KD, P], F32R), sb("w_lo", [P, 2, KD, P], F32R)
        cur = sb("cur", [P, KD, T])
        work = sb("work", [P, 28, T])
        vec = sb("vec", [P, NVEC])
        ones, idn = sb("ones", [P, P]), sb("idn", [P, P])
        small = sb("small", [P, 64])

        h_dram = nc.dram_tensor("h_dram", [P, KD, T], F32, kind="Internal").ap()
        gelu_dram = nc.dram_tensor("gelu_dram", [NKEYS, P, T], F32, kind="Internal").ap()
        gate_dram = nc.dram_tensor("gate_dram", [U2, P, NKEYS * TB], F32, kind="Internal").ap()

        s_raw = [sem("s_raw0"), sem("s_raw1")]
        s_hi, s_lo = sem("s_hi"), sem("s_lo")
        s_jobmm, s_jobev = sem("s_jobmm"), sem("s_jobev")
        s_const, s_ones, s_mask = sem("s_const"), sem("s_ones"), sem("s_mask")
        s_x = [sem(f"s_x{q}") for q in range(4)]
        s_sq, s_add, s_ssmm, s_rinv, s_r = sem("s_sq"), sem("s_add"), sem("s_ssmm"), sem("s_rinv"), sem("s_r")
        s_n, s_nhi, s_nlo = sem("s_n"), sem("s_nhi"), sem("s_nlo")
        s_vec, s_act = sem("s_vec"), sem("s_act")
        s_take = sem("s_take")
        s_up, s_z, s_zb, s_ln, s_cum, s_exc, s_e, s_dec = [sem(n) for n in (
            "s_up", "s_z", "s_zb", "s_ln", "s_cum", "s_exc", "s_e", "s_dec")]
        s_qk, s_vtp, s_vt, s_att, s_ate, s_atm, s_ats, s_ktp, s_kt = [sem(n) for n in (
            "s_qk", "s_vtp", "s_vt", "s_att", "s_ate", "s_atm", "s_ats", "s_ktp", "s_kt")]
        s_kv, s_st, s_o, s_osq, s_oss, s_ginv, s_gr, s_sil, s_y = [sem(n) for n in (
            "s_kv", "s_st", "s_o", "s_osq", "s_oss", "s_ginv", "s_gr", "s_sil", "s_y")]
        s_tab = sem("s_tab")
        s_avp, s_av, s_qkm, s_sb, s_p, s_ptp, s_pt, s_pv, s_nrm, s_otp, s_ot = [sem(n) for n in (
            "s_avp", "s_av", "s_qkm", "s_sb", "s_p", "s_ptp", "s_pt", "s_pv", "s_nrm", "s_otp", "s_ot")]
        s_half, s_halfev = sem("s_half"), sem("s_halfev")
        s_xr, s_hsaved = [sem("s_xr0"), sem("s_xr1")], sem("s_hsaved")
        s_keys, s_scp, s_sc = sem("s_keys"), sem("s_scp"), sem("s_sc")
        s_apart = sem("s_apart")
        s_tke, s_tkx, s_route, s_rtp, s_rt = sem("s_tke"), sem("s_tkx"), sem("s_route"), sem("s_rtp"), sem("s_rt")
        s_gst, s_gd = [sem(f"s_gst{n}") for n in range(4)], [sem(f"s_gd{n}") for n in range(2)]
        s_hot, s_gmm, s_gev = sem("s_hot"), sem("s_gmm"), sem("s_gev")
        s_v, s_a, s_g = [sem(f"s_v{n}") for n in range(VG)], [sem(f"s_a{n}") for n in range(VG)], [sem("s_g0"), sem("s_g1")]
        s_vh, s_vl, s_w, s_wh, s_wl, s_vmm = [sem(n) for n in ("s_vh", "s_vl", "s_w", "s_wh", "s_wl", "s_vmm")]
        s_hl, s_vend, s_vev, s_fin, s_out = sem("s_hl"), sem("s_vend"), sem("s_vev"), sem("s_fin"), sem("s_out")

        block = ctx.enter_context(nc.Block())

        up, gates_in = sb("up", [32 + RANK, DK]), sb("gates_in", [P, T])
        gd, gup = gates_in[0:32 + RANK], gates_in[64:96 + RANK]
        bias, dec, slope = small[:, 0:2], small[:, 2:18].rearrange("p (d n) -> p d n", d=2), small[:, 18:22]
        negmax, rden = small[:, 22:24], small[:, 24:25]

        fresh, taken = work[:, 0:6], work[:, 6:12]
        n_tmp = work[:, 6:8]
        sq_tmp, sq_sum, r_t = [(x, x, x, y) for x, y in (
            (work[:, 8:12:3], work[:, 12:14]), (work[:, 4], work[:, 14]), (work[:, 5], work[:, 15]))]
        zb, ab, la, cum, exc = [work[:, 12 + n] for n in range(5)]
        qd, kd, ke, mask = work[:, 17:19], work[:, 19:21], work[:, 21], work[:, 22]
        kt = work[:, 23:25]
        vt = work[:, 25:27].rearrange("p a (b e) -> p (a b) e", e=DV)
        at = work[:, 27].rearrange("p (d a c) -> p d a c", d=2, c=CHUNK)
        at_sum = sb("at_sum", [P, NC // 2, P])
        osq, sil, g_r, g_ri = work[:, 19:21], work[:, 12:14], work[:, 14], work[:, 15]
        state = cur[:, 8:16]
        logit, prob, prob_t = work[:, 12:14], work[:, 14:16], work[:, 16:18]
        dist_t = work[:, 18:22]
        count_t = work[:, 22].bitcast(U8).rearrange("p (b t) -> p b t", t=T)
        va = work[:, 24:27].rearrange("p a b -> p (a b)")[:, 0:16 * (HD + 1)].rearrange(
            "p (r s h e) -> p r s h e", r=2, s=TT, h=2)
        att_rows = work[:, 27].rearrange("p (a e) -> p a e", e=P)
        x_res = work[:, 12:14]
        partial = [cur[:, m] for m in range(HK)] + [work[:, m] for m in range(4)] + [
            at_sum[:, :, :].rearrange("p a c -> p (a c)"), gates_in[:, :]]
        q_t, keys = work[:, 14:16], work[:, 16:20].rearrange("p a b -> p (a b)").rearrange("p (n k) -> p n k", k=NKEYS)
        score_t = cur[:, :].rearrange("p a b -> p (a b)")
        gelu_t = work[:, 0:4]
        tk_in, tk_cut = [work[:, 4, 256 * n:256 * n + 256].rearrange("p (c k) -> p c k", c=2) for n in range(2)]
        pair_sum, pair_cut = work[:, 5, 0:256], work[:, 5, 256:512]
        picked, chosen = [work[:, 6, 256 * n:256 * n + 256].rearrange("p (a b) -> p a b", b=TOPK) for n in range(2)]
        tiny = work[:, 7].rearrange("p (n k) -> p n k", k=TOPK)
        val, idx, idx_f = tiny[:, 0:2], tiny[:, 2:4].bitcast(U32), tiny[:, 4:6]
        top, place, place_2, place_f = tiny[:, 6:8], tiny[:, 8].bitcast(U32), tiny[:, 9:11].bitcast(U32), tiny[:, 11:13]
        top_exp, tk_neg, tk_sum, tk_inv = tiny[:, 13:15], tiny[:, 15, 0:2], tiny[:, 15, 2:4], tiny[:, 15, 4:6]
        count_up = work[:, 19, T - NKEYS:T]
        routed = work[:, 9:12]
        routed_t = work[:, 12:15]
        hot2 = work[:, 15:17].rearrange("p a b -> p (a b)").rearrange("p (n k) -> p n k", k=NKEYS)
        hot1 = work[:, 17:19].rearrange("p a b -> p (a b)").rearrange("p (n k) -> p n k", k=NKEYS)
        route_tb = work[:, 19, 0:6 * TB].rearrange("p (r x t) -> p r x t", r=2, x=3)
        gate_t = cur[:, :].rearrange("p (r a) t -> p r (a t)", r=2).rearrange("p r (i t) -> p r i t", t=TB)
        g_t = [work[:, a:a + 4].rearrange("p a t -> p (a t)").rearrange("p (b e t) -> p b e t", b=U2, e=VG) for a in (4, 0)]
        a_t, weight_t = work[:, 8:12], work[:, 16:18]
        v_raw = work[:, 20:28].rearrange("p a t -> p (a t)").rearrange("p (n c) -> p n c", c=HALF)
        v_hi, v_lo = [x[:, :, :].rearrange("p a t -> p (a t)").rearrange("p (n c) -> p n c", c=HALF) for x in (act_hi, act_lo)]
        g_hi, g_lo = [x[:, :, :, :].rearrange("p s k c -> p (s k c)").rearrange("p (n t) -> p n t", t=T) for x in (w_hi, w_lo)]

        @block.sync
        def _(sp):
            for n in range(2):
                sp.dma_start(raw[:, n], weights[n].rearrange("p (k c) -> p k c", c=P)).then_inc(s_raw[n], 16)
            last = NJOBS
            with sp.Fori(0, (last - 3) // 2) as i:
                for j in range(2):
                    J = job(2, 2, i, j)
                    sp.wait_ge(s_lo, J.n - 1)
                    sp.dma_start(raw[:, J.slot], weights[bass.ds(J.n, 1)].rearrange("o p (k c) -> p (o k) c", c=P)
                                 ).then_inc(s_raw[J.slot], 16)
            for n in range(2 + 2 * ((last - 3) // 2), last):
                sp.wait_ge(s_lo, n - 1)
                sp.dma_start(raw[:, n % 2], weights[n].rearrange("p (k c) -> p k c", c=P)).then_inc(s_raw[n % 2], 16)


            def v_tile(half, i, r, e, early):
                n = NKEYS * half + 8 * i + 4 * r + e
                if not early:
                    sp.wait_ge(s_vl, n - 3)
                rows = bass.ds(8 * i + 4 * r + e, 1)
                sp.dma_start(v_raw[:, e], peer_v.rearrange("(m p) d -> m p d", p=P)[rows, :, HALF * half:HALF * (half + 1)]
                             .rearrange("o p d -> p (o d)")).then_inc(s_v[e], 16)

            def w_tiles(half, i, r, first):
                n = NKEYS * half + 8 * i + 4 * r
                if not first:
                    sp.wait_ge(s_w, n - 4)
                m = (8 * i + 4 * r) * TB
                sp.dma_start(g_t[r].rearrange("p b e t -> p b (e t)"),
                             gate_dram[:, :, bass.ds(m, VG * TB)].rearrange("b p c -> p b c")).then_inc(s_g[r], 16)

            def a_tile(half, i, r, e, first):
                n = NKEYS * half + 8 * i + 4 * r + e
                if not first:
                    sp.wait_ge(s_w, n - 3)
                sp.dma_start(a_t[:, e], gelu_dram[bass.ds(8 * i + 4 * r + e, 1)].rearrange("o p t -> p (o t)")
                             ).then_inc(s_a[e], 16)

            sp.wait_ge(s_sc, 2 * PEER_HEADS)
            for e in range(VG):
                v_tile(0, 0, 0, e, True)
            for e in range(VG):
                sp.wait_ge(s_gst[e], 16 * (U1 + U2 - 1))
            sp.wait_ge(s_rtp, 3)
            for e in range(VG):
                a_tile(0, 0, 0, e, True)
            sp.wait_ge(s_gd[0], 16 * U2 // 2)
            sp.wait_ge(s_gd[1], 16 * (U2 // 2 - 1))
            sp.dma_start(g_t[0][:, 0:U2 - 1].rearrange("p b e t -> p b (e t)"),
                         gate_dram[0:U2 - 1, :, 0:VG * TB].rearrange("b p c -> p b c")).then_inc(s_g[0], 16)
            for e in range(VG):
                sp.wait_ge(s_gst[e], 16 * (U1 + U2))
            sp.wait_ge(s_gd[1], 16 * U2 // 2)
            for half in range(2):
                def v_round(i, first=False):
                    for r in range(2):
                        if first and r == 0:
                            continue
                        w_tiles(half, i, r, first)
                        for e in range(VG):
                            a_tile(half, i, r, e, False)
                            v_tile(half, i, r, e, False)
                if half == 0:
                    v_round(0, True)
                    for k in range(2):
                        sp.dma_start(cur[:, 8 * k:8 * k + 8], h_dram[:, 8 * k:8 * k + 8]).then_inc(s_hl, 16)
                with sp.Fori(1 - half, VR // 2) as i:
                    v_round(i)

        @block.gpsimd
        def _(pool):
            for q in range(4):
                pool.dma_start(cur[:, 4 * q:4 * q + 4], x_t[:, 4 * q:4 * q + 4]).then_inc(s_x[q], 16)
                if q == 0:
                    pool.dma_start(vec[:, :], vectors).then_inc(s_const, 16)
                    pool.dma_start(idn[:, :], ident).then_inc(s_const, 16)
            pool.dma_start(gup, gate_up).then_inc(s_const, 16)
            pool.dma_start(mask, scan_mask).then_inc(s_const, 16)
            with pool.Fori(0, NGLA) as h:
                for d in range(2):
                    pool.wait_ge(s_ate, 2 * h + d + 1)
                    pool.sem_inc(s_mask, 1)
                    for half in range(2):
                        a = at[64 * half:64 * half + 64, d]
                        nc.gpsimd.affine_select(
                            out=a, in_=a, compare_op=ALU.is_ge, fill=0.0, base=0,
                            pattern=[[0, NC // 2], [1 - 2 * d, CHUNK]], channel_multiplier=2 * d - 1,
                        ).then_inc(s_atm, 1)
            pool.wait_ge(s_y, 2 * NGLA)
            pool.dma_start(dist_t, dist).then_inc(s_tab, 16)
            pool.dma_start(work[:, 12:16], count).then_inc(s_tab, 16)
            pool.wait_ge(s_p, 16 * NATT)
            for n in range(2):
                pool.dma_start(x_res[:, n], x_t[:, 2 * NPAIR + n]).then_inc(s_xr[n], 16)
            for n in range(2):
                pool.wait_ge(s_jobev, JOB_WHOLE + n + 1)
                pool.dma_start(x_res[:, n], x_t[:, n]).then_inc(s_xr[n], 16)
            with pool.Fori(0, NPAIR - 1) as i:
                for j in range(2):
                    if j == 0:
                        pool.wait_ge(s_halfev, i + (NPAIR + 1))
                    else:
                        pool.wait_ge(s_jobev, i + (JOB_ATT + 1))
                    pool.dma_start(x_res[:, j], x_t[:, bass.ds(2 * i + (2 + j), 1)].rearrange("p o t -> p (o t)")
                                   ).then_inc(s_xr[j], 16)
            pool.dma_start(keys, sub_keys).then_inc(s_keys, 16)
            pool.wait_ge(s_jobev, JOB_Q)
            for q in range(4):
                pool.dma_start(h_dram[:, 4 * q:4 * q + 4], cur[:, 4 * q:4 * q + 4]).then_inc(s_hsaved, 16)
            pool.wait_ge(s_hsaved, 64)
            pool.wait_ge(s_sc, 2 * PEER_HEADS)
            pool.dma_start(count_up, steps).then_inc(s_keys, 16)

            def store_gelu(i, j):
                pool.wait_ge(s_jobev, 4 * i + (JOB_U + j + 1))
                pool.dma_start(gelu_dram[bass.ds(4 * i + j, 1)].rearrange("o p t -> p (o t)"), gelu_t[:, j]).then_inc(s_gst[j], 16)

            with pool.Fori(0, U1) as i:
                for j in range(4):
                    store_gelu(i, j)
            with pool.Fori(0, U2 // 2) as i:
                for r in range(2):
                    for j in range(4):
                        store_gelu(2 * i + (U1 + r), j)
                    pool.wait_ge(s_gev, 16 * i + 8 * r + 8 + BANKS_FREE)
                    pool.dma_start(gate_dram[bass.ds(2 * i + r, 1)].rearrange("o p c -> p (o c)"),
                                   gate_t[:, r].rearrange("p i t -> p (i t)")).then_inc(s_gd[r], 16)
            for q in range(4):
                pool.wait_ge(s_fin, 4 * q + 4)
                pool.dma_start(out_t.rearrange("(k p) t -> p k t", p=P)[:, 4 * q:4 * q + 4], cur[:, 4 * q:4 * q + 4]
                               ).then_inc(s_out, 16)
            pool.wait_ge(s_out, 64)

        @block.scalar
        def _(act):
            link = Chain(act, s_act)
            act.sem_inc(s_gev, BANKS_FREE)

            def split(J, first=False):
                act.wait_ge(s_raw[J.slot], 16 * (J.use + 1))
                if not first:
                    act.wait_ge(s_jobmm, J.n - 1)
                nc.scalar.copy(w_hi[:, J.slot], raw[:, J.slot]).then_inc(s_hi, 1)

            def evacuate(J, dst, rows=P):
                act.wait_ge(s_jobmm, J.n + 1)
                nc.scalar.copy(dst, psum[0:rows, J.slot]).then_inc(s_jobev, 1)

            def square(stage, k, slot, src):
                if not (isinstance(k, int) and k < SQ_BASE[stage] + 2):
                    act.wait_ge(s_add, k - 1)
                nc.scalar.activation(sq_tmp[stage][:, slot], src, ACT.Square).then_inc(s_sq, 1)

            def root(stage):
                act.wait_ge(s_rinv, stage + 1)
                nc.scalar.activation(r_t[stage], sq_sum[stage], ACT.Sqrt).then_inc(s_r, 1)

            def halves(k, src, made):
                if made:
                    act.wait_ge(s_n, made)
                nc.scalar.copy(act_hi[:, k], src).then_inc(s_nhi, 1)

            split(job(0, 0, 0, 0), True)
            for k in range(KD):
                act.wait_ge(s_x[k // 4], 16)
                square(0, k, k % 2, cur[:, k])
            root(0)
            for k in range(KD):
                halves(k, n_tmp[:, k % 2], k + 1)
            split(job(1, 0, 0, 0), True)
            evacuate(job(0, 0, 0, 0), gd, 32 + RANK)
            for j in range(GROUP):
                J = job(JOB_GROUPS, 0, 0, j)
                split(job(JOB_GROUPS + 1, 0, 0, j))
                evacuate(J, fresh[:, j])

            def next_jobs(p, first, i, groups_taken, more=True):
                if p % 3 == 0:
                    j = p // 3
                    if j:
                        evacuate(job(first, GROUP, i, j - 1), fresh[:, j - 1])
                    if j == 0:
                        act.wait_ge(s_take, groups_taken)
                    if j < GROUP and (more or j < GROUP - 1):
                        split(job(first + 1, GROUP, i, j))

            with act.Fori(0, NGLA) as h:
                link.enter(h, 4)

                def gates(d):
                    act.wait_ge(s_zb, 2 * h + d + 1)
                    link(nc.scalar.activation(ab, zb, ACT.Abs))
                    link(nc.scalar.activation(ab, ab, ACT.Exp, scale=-1.0))
                    nc.scalar.activation(ab, ab, ACT.Ln, bias=1.0).then_inc(s_ln, 1)

                def exps(d):
                    act.wait_ge(s_cum, 2 * h + d + 1)
                    b = (cum, la)[d]
                    nc.scalar.activation(zb, b, ACT.Exp, scale=1.0 / TAU).then_inc(s_e, 1)
                    nc.scalar.activation(ab, b, ACT.Exp, scale=-1.0 / TAU).then_inc(s_e, 1)
                    nc.scalar.activation(dec[:, d], cum.rearrange("p (n c) -> p n c", c=CHUNK)[:, :, CHUNK - 1],
                                         ACT.Exp, scale=1.0 / TAU).then_inc(s_dec, 1)
                    if d == 0:
                        act.wait_ge(s_exc, h + 1)
                    nc.scalar.activation(exc, exc, ACT.Exp, scale=1.0 / TAU).then_inc(s_e, 1)

                def v_rows():
                    act.wait_ge(s_vtp, h + 1)
                    for t in range(DVT):
                        nc.scalar.copy(vt[:, :, t * P:(t + 1) * P],
                                       psum[:, 5 + t].rearrange("p (a e) -> p a e", e=P)).then_inc(s_vt, 1)

                def scores(d):
                    act.wait_ge(s_att, 2 * h + d + 1)
                    nc.scalar.copy(at[:, d].rearrange("p a c -> p (a c)"), psum[:, 4, 256 * d:256 * d + 256]).then_inc(s_ate, 1)
                    act.wait_ge(s_ktp, 2 * h + d + 1)
                    nc.scalar.copy(kt[:, d], psum[:, 2 + d]).then_inc(s_kt, 1)

                def silu():
                    nc.scalar.activation(sil, taken[:, 4:6], ACT.Silu).then_inc(s_sil, 1)

                def squares():
                    for t in range(DVT):
                        act.wait_ge(s_o, 2 * h + t + 1)
                        nc.scalar.activation(osq[:, t], psum[:, 5 + t], ACT.Square).then_inc(s_osq, 1)

                def head_root():
                    act.wait_ge(s_ginv, h + 1)
                    nc.scalar.activation(g_r, g_ri, ACT.Sqrt).then_inc(s_gr, 1)

                at_part = {0: lambda: gates(0), 1: v_rows, 2: lambda: exps(0), 4: lambda: gates(1), 6: lambda: scores(0),
                           5: lambda: exps(1), 8: lambda: scores(1), 9: silu, 14: squares, 15: head_root}
                for p in range(PARTS):
                    next_jobs(p, JOB_GROUPS + GROUP, h, h + 1)
                    if p in at_part:
                        at_part[p]()
                evacuate(job(JOB_GROUPS + GROUP, GROUP, h, GROUP - 1), fresh[:, GROUP - 1])
                link.leave(NGLA)

            def half_sum(n):
                if n == 0:
                    act.wait_ge(s_take, NGLA + NATT)
                    act.wait_ge(s_nlo, KD + HK)
                if n % 2 == 0:
                    act.wait_ge(s_half, n // 2 + 1)
                    nc.scalar.copy(partial[n], psum[:, 0]).then_inc(s_halfev, 1)
                else:
                    act.wait_ge(s_jobmm, JOB_OUT + n // 2 + 1)
                    nc.scalar.copy(partial[n], psum[:, 1]).then_inc(s_jobev, 1)

            def attention(g, first, i, jobs, more=True):
                for p in range(PARTS):
                    if jobs:
                        next_jobs(p, first, i, NGLA + g + 1, more)
                    n = p - PAIR_PART
                    if not jobs and 0 <= n < 2 * NPAIR and n % 2 == 0:
                        split(job(JOB_OUT + 1, 0, 0, n // 2))
                    if not jobs and 1 <= n <= 2 * NPAIR:
                        half_sum(n - 1)
                    if p < 16:
                        act.wait_ge(s_sb, 16 * g + p + 1)
                        if p >= 2:
                            act.wait_ge(s_ptp, 16 * g + p - 1)
                        nc.scalar.activation(prob[:, p % 2], logit[:, p % 2], ACT.Exp,
                                             bias=negmax[:, p % 2:p % 2 + 1]).then_inc(s_p, 1)
                    if not jobs:
                        if p == 0:
                            act.wait_ge(s_take, NGLA + NATT)
                            act.wait_ge(s_ot, 2 * NATT - 2)
                        if p in Y_SQUARES:
                            if p == Y_SQUARES[6]:
                                act.wait_ge(s_ot, 2 * NATT - 1)
                            square(1, KD + Y_SQUARES.index(p), Y_SQUARES.index(p) % 2, cur[:, HK + Y_SQUARES.index(p)])
                        for k in range(HK):
                            if Y_HALVES[k] == p:
                                halves(k, cur[:, k], 0)
                if jobs:
                    evacuate(job(first, GROUP, i, GROUP - 1), fresh[:, GROUP - 1])

            first = JOB_GROUPS + GROUP * (NGLA + 1)
            with act.Fori(0, NATT - 1) as g:
                attention(g, first, g, True)
            attention(NATT - 1, 0, 0, False)

            act.wait_ge(s_ot, 2 * NATT)
            square(1, KD + 7, 1, cur[:, KD - 1])
            split(job(JOB_WHOLE + 1, 0, 0, 0))
            root(1)
            for k in range(8, KD):
                halves(k, n_tmp[:, k % 2], KD + k - 7)
            for n in range(2):
                split(job(JOB_WHOLE + 2, 0, 0, n))
                act.wait_ge(s_jobev, JOB_WHOLE + n + 1)
                square(2, SQ_BASE[2] + n, n, cur[:, 2 * NPAIR + n])

            def pair_squares(i, a):
                for j in range(2):
                    if j == 0:
                        act.wait_ge(s_halfev, 2 * i + (NPAIR + a + 1))
                    else:
                        act.wait_ge(s_jobev, 2 * i + (JOB_ATT + a + 1))
                    square(2, 4 * i + (SQ_BASE[2] + 2 + 2 * a + j), j,
                           cur[:, bass.ds(4 * i + (2 * a + j), 1)].rearrange("p o t -> p (o t)"))

            with act.Fori(0, NPAIR // 2) as i:
                for a in range(2):
                    pair_squares(i, a)
                    split(job(JOB_ATT + 2, 2, i, a))
            for j in range(2):
                if j == 0:
                    act.wait_ge(s_halfev, 2 * NPAIR)
                else:
                    act.wait_ge(s_jobev, JOB_Q)
                square(2, SQ_BASE[2] + KD - 2 + j, j, cur[:, 2 * NPAIR - 2 + j])
            root(2)
            for k in range(KD):
                halves(k, n_tmp[:, k % 2], KD + 8 + k + 1)

            act.wait_ge(s_hsaved, 64)
            with act.Fori(0, PEER_HEADS) as i:
                for j in range(2):
                    split(job(JOB_Q + 1, 2, i, j))
                    evacuate(job(JOB_Q, 2, i, j), q_t[:, j])
                    act.wait_ge(s_scp, 2 * i + j + 1)
                    nc.scalar.copy(cur[:, :].rearrange("p (a q) t -> p a (q t)", a=TT)[:, :, bass.ds(2 * P * i + P * j, P)],
                                   psum[:, 2 + j].rearrange("p (a k) -> p a k", k=NKEYS)).then_inc(s_sc, 1)

            def gelu(J, j, stores):
                act.wait_ge(s_jobmm, J.n + 1)
                if stores is not None:
                    act.wait_ge(s_gst[j], 16 * stores)
                nc.scalar.activation(gelu_t[:, j], psum[:, J.slot], ACT.Gelu).then_inc(s_jobev, 1)

            def u1_round(i, first=False):
                for j in range(4):
                    split(job(JOB_U + 1, 4, i, j))
                    gelu(job(JOB_U, 4, i, j), j, None if first else i)
                    if j == 3:
                        for u in range(2):
                            act.wait_ge(s_tke, 2 * i + u + 1)
                            nc.scalar.activation(top_exp[:, u], top[:, u], ACT.Exp, bias=tk_neg[:, u:u + 1],
                                                 accum_out=tk_sum[:, u:u + 1]).then_inc(s_tkx, 1)

            u1_round(0, first=True)
            with act.Fori(1, U1) as i:
                u1_round(i)
            for x in range(3):
                act.wait_ge(s_rtp, x + 1)
                nc.scalar.copy(routed_t[:, x], psum[:, 2 + x]).then_inc(s_rt, 1)

            def u2_round(i, first=False, last=False):
                for r in range(2):
                    for j in range(4):
                        if not (last and r == 1 and j == 3):
                            split(job(JOB_U + 4 * U1 + 1, 8, i, 4 * r + j))
                        for q in (2 * j, 2 * j + 1):
                            act.wait_ge(s_gmm, 16 * i + 8 * r + q + 1 + HOT_FREE)
                            if q == 0 and not first:
                                act.wait_ge(s_gd[r], 16 * i)
                            nc.scalar.copy(gate_t[:, r, :, 4 * q:4 * q + 4],
                                           psum[:, 2 + q % 4].rearrange("p (t k) -> p k t", k=NKEYS)).then_inc(s_gev, 1)
                        gelu(job(JOB_U + 4 * U1, 8, i, 4 * r + j), j, 2 * i + (U1 + r))

            u2_round(0, first=True)
            with act.Fori(1, U2 // 2 - 1) as i:
                u2_round(i)
            u2_round(U2 // 2 - 1, last=True)
            act.wait_ge(s_jobmm, NJOBS)

            def v_highs(half, i, r, e, early=False):
                n = NKEYS * half + 8 * i + 4 * r + e
                act.wait_ge(s_v[e], 16 * (2 * i + (32 * half + r + 1)))
                if not early:
                    act.wait_ge(s_vmm, n - 3)
                nc.scalar.copy(v_hi[:, e], v_raw[:, e]).then_inc(s_vh, 1)
                act.wait_ge(s_w, n + 1)
                nc.scalar.copy(g_hi[:, e], weight_t[:, e % 2]).then_inc(s_wh, 1)

            for half in range(2):
                for r in range(2):
                    for e in range(VG):
                        v_highs(half, 0, r, e, half == 0 and r == 0)
                        if half:
                            m = VG * r + e
                            act.wait_ge(s_vev, m + 1)
                            square(3, SQ_BASE[3] + m, m % 2, cur[:, m])
                with act.Fori(1, VR // 2) as i:
                    for r in range(2):
                        for e in range(VG):
                            v_highs(half, i, r, e)
            for m in range(HT, KD):
                act.wait_ge(s_vev, m + 1)
                square(3, SQ_BASE[3] + m, m % 2, cur[:, m])
            root(3)

        @block.tensor
        def _(pe):
            def products(o, slot, shift, ks, first_k, last_k, ready=None):
                for k in ks:
                    if ready:
                        ready(k)
                    nc.tensor.matmul(o, w_hi[:, slot, k + shift], act_hi[:, k], start=(k == first_k), stop=False)
                    nc.tensor.matmul(o, w_hi[:, slot, k + shift], act_lo[:, k], start=False, stop=False)
                    last = nc.tensor.matmul(o, w_lo[:, slot, k + shift], act_hi[:, k], start=False, stop=(k == last_k))
                return last

            def part(J, third, first=False, ready=None):
                if third == 0:
                    pe.wait_ge(s_lo, J.n + 1)
                    if not first:
                        pe.wait_ge(s_jobev, J.n - 1)
                last = products(psum[:, J.slot], J.slot, 0, range(CUT[third], CUT[third + 1]), 0, KD - 1, ready)
                if third == 2:
                    last.then_inc(s_jobmm, 1)

            def whole(J, first=False, ready=None):
                for third in range(3):
                    part(J, third, first, ready)

            def sum_squares(stage):
                pe.wait_ge(s_add, (*SQ_BASE[1:], 3 * KD + 8)[stage])
                nc.tensor.matmul(psum[:, 2], ones[:, :], sq_sum[stage], start=True, stop=True).then_inc(s_ssmm, 1)

            def tile_halves(stage, k):
                pe.wait_ge(s_nlo, stage * KD + k + 1)

            pe.sem_inc(s_gmm, HOT_FREE)
            pe.wait_ge(s_ones, 1)
            sum_squares(0)
            whole(job(0, 0, 0, 0), True, lambda k: tile_halves(0, k))
            pe.wait_ge(s_const, 64)
            for j in range(GROUP):
                whole(job(JOB_GROUPS, 0, 0, j), j == 0)

            with pe.Fori(0, NGLA) as h:
                def z():
                    pe.wait_ge(s_up, h + 1)
                    for d in range(2):
                        r = slice(32 * d, 32 * d + RANK)
                        nc.tensor.matmul(psum[:, 2 + d], up[r, :], gd[r, :], start=True, stop=True).then_inc(s_z, 1)

                def v_rows():
                    pe.wait_ge(s_take, h + 1)
                    for t in range(DVT):
                        for a in range(TT):
                            last = nc.tensor.transpose(psum[:, 5 + t, a * P:(a + 1) * P], taken[:, 2 + t, a * P:(a + 1) * P],
                                                       idn[:, :])
                    last.then_inc(s_vtp, 1)

                def scores(d):
                    pe.wait_ge(s_qk, 6 * h + 3 * d + 3)
                    if d:
                        pe.wait_ge(s_ate, 2 * h + 1)
                    for c in range(NC):
                        t = slice(CHUNK * c, CHUNK * (c + 1))
                        o = psum[64 * (c % 2):64 * (c % 2) + 64, 4, 256 * d + CHUNK * (c // 2):256 * d + CHUNK * (c // 2 + 1)]
                        last = nc.tensor.matmul(o, kd[:, d, t], qd[:, d, t], start=True, stop=True)
                    last.then_inc(s_att, 1)
                    for a in range(TT):
                        last = nc.tensor.transpose(psum[:, 2 + d, a * P:(a + 1) * P], ke[:, a * P:(a + 1) * P], idn[:, :])
                    last.then_inc(s_ktp, 1)

                def kv(n0, n1):
                    for n in range(n0, n1):
                        d, step = n % 2, n // 2
                        c = step if d == 0 else NC - 1 - step
                        if n == 0:
                            pe.wait_ge(s_kt, 2 * h + 2)
                            pe.wait_ge(s_ate, 2 * h + 2)
                            pe.wait_ge(s_vt, 2 * h + 2)
                        if n >= 4:
                            pe.wait_ge(s_st, 14 * h + n - 3)
                        r = slice(64 * (c % 2), 64 * (c % 2) + 64)
                        nc.tensor.matmul(psum[:, KV_BANKS[n % 4], 0:DV],
                                         kt[r, d, (c // 2) * P:(c // 2 + 1) * P], vt[r, c // 2, :],
                                         start=True, stop=True).then_inc(s_kv, 1)

                def outputs():
                    pe.wait_ge(s_ats, 2 * h + 2)
                    pe.wait_ge(s_st, 14 * h + 14)
                    for t in range(DVT):
                        for a in range(NC // 2):
                            pair = slice(P * a, P * (a + 1))
                            nc.tensor.matmul(psum[:, 5 + t, pair], vt[:, a, t * P:(t + 1) * P], at_sum[:, a, :],
                                             start=True, stop=False)
                            for c in (2 * a, 2 * a + 1):
                                for d in range(2):
                                    if (c, d) in ((0, 0), (NC - 1, 1)):
                                        continue
                                    cols = slice(CHUNK * c, CHUNK * (c + 1))
                                    last = nc.tensor.matmul(
                                        psum[:, 5 + t, cols], state[:, c, DV * d + t * P:DV * d + (t + 1) * P], qd[:, d, cols],
                                        start=False, stop=(c % 2 == 1 and (d == 1 or c == NC - 1)))
                        last.then_inc(s_o, 1)

                def mean_square():
                    for t in range(DVT):
                        pe.wait_ge(s_osq, 2 * h + t + 1)
                        last = nc.tensor.matmul(psum[:, 2], ones[:, :], osq[:, t], start=(t == 0), stop=(t == DVT - 1))
                    last.then_inc(s_oss, 1)

                at_part = {0: z, 1: v_rows, 5: lambda: scores(0), 7: lambda: scores(1), 8: lambda: kv(0, 4),
                           9: lambda: kv(4, 8), 10: lambda: kv(8, 12), 11: lambda: kv(12, 14), 13: outputs, 14: mean_square}
                for p in range(PARTS):
                    part(job(JOB_GROUPS + GROUP, GROUP, h, p // 3), p % 3)
                    if p in at_part:
                        at_part[p]()

            def attention(g, first, i, jobs):
                def v_rows(pr):
                    if pr == 0:
                        pe.wait_ge(s_take, NGLA + g + 1)
                    for a in range(TT):
                        last = nc.tensor.transpose(psum[:, 7 - pr, a * P:(a + 1) * P], taken[:, 3 * pr + 2, a * P:(a + 1) * P],
                                                   idn[:, :])
                    last.then_inc(s_avp, 1)

                def out_rows(pr):
                    pe.wait_ge(s_nrm, 16 * g + 8 * pr + 8)
                    if pr == 0:
                        pe.wait_ge(s_av, 2 * g + 1)
                    else:
                        pe.wait_ge(s_ot, 2 * g + 1)
                    for a in range(TT):
                        last = nc.tensor.transpose(psum[:, 7, a * P:(a + 1) * P], att_rows[:, a, :], idn[:, :])
                    last.then_inc(s_otp, 1)

                for p in range(PARTS):
                    if jobs:
                        part(job(first, GROUP, i, p // 3), p % 3)
                    n = p - PAIR_PART
                    if not jobs and 0 <= n < 2 * NPAIR:
                        if n % 2 == 0:
                            pe.wait_ge(s_lo, JOB_OUT + n // 2 + 1)
                        if n < 2:
                            pe.wait_ge(s_jobev, JOB_OUT)
                        elif n % 2 == 0:
                            pe.wait_ge(s_halfev, n // 2)
                        else:
                            pe.wait_ge(s_jobev, JOB_OUT + n // 2)
                        products(psum[:, n % 2], (JOB_OUT + n // 2) % 2, HK * (n % 2), range(HK), 0, HK - 1,
                                 (lambda k: tile_halves(1, k)) if n == 0 else None
                                 ).then_inc(s_jobmm if n % 2 else s_half, 1)
                    if p == 0:
                        v_rows(0)
                        v_rows(1)
                    if p < 16:
                        pr, hd, a = p // 8, (p // 4) % 2, p % 4
                        r = slice(HD * hd, HD * hd + HD)
                        nc.tensor.matmul(psum[:, 2 + p % 2], taken[r, 3 * pr, a * P:(a + 1) * P], taken[r, 3 * pr + 1, :],
                                         start=True, stop=True).then_inc(s_qkm, 1)
                    if 1 <= p <= 16:
                        u = p - 1
                        pe.wait_ge(s_p, 16 * g + u + 1)
                        if u >= 2:
                            pe.wait_ge(s_pt, 16 * g + u - 1)
                        for s in range(TT):
                            last = nc.tensor.transpose(psum[:, 4 + u % 2, s * P:(s + 1) * P], prob[:, u % 2, s * P:(s + 1) * P],
                                                       idn[:, :])
                        last.then_inc(s_ptp, 1)
                    if p == 10:
                        out_rows(0)
                    if p >= 2:
                        u = p - 2
                        pr, hd = u // 8, (u // 4) % 2
                        pe.wait_ge(s_pt, 16 * g + u + 1)
                        if u == 0:
                            pe.wait_ge(s_av, 2 * g + 2)
                        if u >= 1:
                            pe.wait_ge(s_nrm, 16 * g + u)
                        for s in range(TT):
                            last = nc.tensor.matmul(psum[:, 6, (u % 2) * P:(u % 2) * P + HD + 1],
                                                    prob_t[:, u % 2, s * P:(s + 1) * P], va[:, pr, s, hd, :],
                                                    start=(s == 0), stop=(s == TT - 1))
                        last.then_inc(s_pv, 1)
                out_rows(1)

            first = JOB_GROUPS + GROUP * (NGLA + 1)
            with pe.Fori(0, NATT - 1) as g:
                attention(g, first, g, True)
            attention(NATT - 1, 0, 0, False)

            for n in range(2):
                pe.wait_ge(s_lo, JOB_WHOLE + n + 1)
                if n:
                    pe.wait_ge(s_jobev, JOB_WHOLE)
                    sum_squares(1)
                else:
                    pe.wait_ge(s_halfev, NPAIR)
                products(psum[:, n], n, 0, range(HK), 0, KD - 1)
            for n in range(2):
                products(psum[:, n], n, 0, range(HK, KD), 0, KD - 1, lambda k: tile_halves(1, k)).then_inc(s_jobmm, 1)

            def pair(i, a):
                for j in range(2):
                    if j == 0:
                        pe.wait_ge(s_lo, 2 * i + (JOB_ATT + a + 1))
                        pe.wait_ge(s_jobev, 2 * i + (JOB_WHOLE + 1 + a))
                        pe.wait_ge(s_halfev, 2 * i + (NPAIR + a))
                    else:
                        pe.wait_ge(s_jobev, 2 * i + (JOB_ATT + a))
                    products(psum[:, j], a, HK * (j - 1), range(HK, KD), HK, KD - 1
                             ).then_inc(s_jobmm if j else s_half, 1)

            with pe.Fori(0, NPAIR // 2) as i:
                for a in range(2):
                    pair(i, a)
            pair(NPAIR // 2, 0)
            sum_squares(2)

            def key_scores(i, j):
                pe.wait_ge(s_jobev, 2 * i + (JOB_Q + j + 1))
                for a in range(TT):
                    last = nc.tensor.matmul(psum[:, 2 + j, a * P:(a + 1) * P], q_t[:, j, a * P:(a + 1) * P],
                                            keys[:, bass.ds(2 * i + j, 1)].rearrange("p o k -> p (o k)"), start=True, stop=True)
                last.then_inc(s_scp, 1)

            def query_pair(i, ready=None):
                whole(job(JOB_Q, 2, i, 0), ready=ready)
                part(job(JOB_Q, 2, i, 1), 0)
                if ready:
                    pe.wait_ge(s_keys, 16)
                key_scores(i, 0)
                part(job(JOB_Q, 2, i, 1), 1)
                part(job(JOB_Q, 2, i, 1), 2)
                key_scores(i, 1)

            query_pair(0, lambda k: tile_halves(2, k))
            with pe.Fori(1, PEER_HEADS) as i:
                query_pair(i)
            with pe.Fori(0, U1) as i:
                for j in range(4):
                    whole(job(JOB_U, 4, i, j))
            pe.wait_ge(s_route, 6 * U1)
            pe.wait_ge(s_sc, 2 * PEER_HEADS)
            for x in range(3):
                for a in range(TT):
                    last = nc.tensor.transpose(psum[:, 2 + x, a * P:(a + 1) * P], routed[:, x, a * P:(a + 1) * P], idn[:, :])
                last.then_inc(s_rtp, 1)

            def outer(i, r, q):
                n = 16 * i + 8 * r + q
                pe.wait_ge(s_hot, n + 1)
                if r == 0 and q < 4:
                    pe.wait_ge(s_rt, 3)
                pe.wait_ge(s_gev, n - 3 + BANKS_FREE)
                for t in range(4):
                    o = psum[:, 2 + q % 4, t * P:(t + 1) * P]
                    last = nc.tensor.matmul(o, hot2[:, 4 * (q % 2) + t], hot1[:, 4 * (q % 2) + t], start=True, stop=True)
                last.then_inc(s_gmm, 1)

            with pe.Fori(0, U2 // 2) as i:
                for r in range(2):
                    for j in range(4):
                        J = job(JOB_U + 4 * U1, 8, i, 4 * r + j)
                        part(J, 0)
                        outer(i, r, 2 * j)
                        part(J, 1)
                        outer(i, r, 2 * j + 1)
                        part(J, 2)

            def v_products(half, i, r, e, first=False, final=False):
                n = NKEYS * half + 8 * i + 4 * r + e
                pe.wait_ge(s_vl, n + 1)
                pe.wait_ge(s_wl, n + 1)
                for m in range(HT):
                    c = slice(P * m, P * (m + 1))
                    if first and half:
                        pe.wait_ge(s_vev, m + 1)
                    nc.tensor.matmul(psum[:, m], v_hi[:, e, c], g_hi[:, e], start=first, stop=False)
                    nc.tensor.matmul(psum[:, m], v_hi[:, e, c], g_lo[:, e], start=False, stop=False)
                    last = nc.tensor.matmul(psum[:, m], v_lo[:, e, c], g_hi[:, e], start=False, stop=final)
                    if final and m < HT - 1:
                        last.then_inc(s_vend, 1)
                last.then_inc(s_vmm, 1)

            pe.wait_ge(s_jobev, NJOBS)
            pe.wait_ge(s_gev, 8 * U2 + BANKS_FREE)
            for half in range(2):
                def v_round(i, first=False, final=False):
                    for r in range(2):
                        for e in range(VG):
                            v_products(half, i, r, e, first and r == e == 0, final and r == 1 and e == VG - 1)

                v_round(0, first=True)
                with pe.Fori(1, VR // 2 - 1) as i:
                    v_round(i)
                v_round(VR // 2 - 1, final=True)
            pe.wait_ge(s_vev, KD)
            sum_squares(3)

        @block.vector
        def _(vec_e):
            dve = vec_e
            link = Chain(dve, s_vec)

            def rest(J):
                dve.wait_ge(s_hi, J.n + 1)
                nc.vector.tensor_tensor(w_lo[:, J.slot], raw[:, J.slot], w_hi[:, J.slot].bitcast(F32), ALU.subtract
                                        ).then_inc(s_lo, 1)

            def inverse(ms, width, dst, done):
                link(nc.vector.tensor_scalar(dst, ms, 1.0 / width, EPS, ALU.mult, ALU.add))
                nc.vector.reciprocal(dst, dst).then_inc(done, 1)

            def add_square(stage, k, slot):
                dve.wait_ge(s_sq, k + 1)
                if isinstance(k, int) and k == SQ_BASE[stage]:
                    nc.vector.tensor_copy(sq_sum[stage], sq_tmp[stage][:, slot]).then_inc(s_add, 1)
                else:
                    dve.wait_ge(s_add, k)
                    nc.vector.tensor_tensor(sq_sum[stage], sq_sum[stage], sq_tmp[stage][:, slot], ALU.add).then_inc(s_add, 1)

            def rms(stage, width):
                dve.wait_ge(s_ssmm, stage + 1)
                inverse(psum[:, 2], width, sq_sum[stage], s_rinv)
                dve.wait_ge(s_r, stage + 1)

            def low(stage, k, src):
                dve.wait_ge(s_nhi, stage * KD + k + 1)
                nc.vector.tensor_tensor(act_lo[:, k], src, act_hi[:, k].bitcast(F32), ALU.subtract).then_inc(s_nlo, 1)

            def normed(stage, first, col, n_base):
                for k in range(first, KD):
                    if k - first >= 2:
                        dve.wait_ge(s_nlo, stage * KD + k - 1)
                    nc.vector.scalar_tensor_tensor(out=n_tmp[:, k % 2], in0=cur[:, k],
                                                   scalar=vec[:, col + k - first:col + k - first + 1],
                                                   in1=r_t[stage], op0=ALU.mult, op1=ALU.mult).then_inc(s_n, 1)
                    dve.wait_ge(s_n, n_base + k - first + 1)
                    if k > first:
                        low(stage, k - 1, n_tmp[:, (k - 1) % 2])
                low(stage, KD - 1, n_tmp[:, (KD - 1) % 2])

            nc.vector.memset(ones[:, :], 1.0).then_inc(s_ones, 1)
            link(nc.vector.memset(at_sum[:, :, :], 0.0))
            rest(job(0, 0, 0, 0))
            for k in range(KD):
                add_square(0, k, k % 2)
            rms(0, D)
            dve.wait_ge(s_const, 64)
            normed(0, 0, V_N1, 0)
            rest(job(1, 0, 0, 0))
            for j in range(GROUP):
                rest(job(JOB_GROUPS + 1, 0, 0, j))

            with dve.Fori(0, NGLA) as h:
                link.enter(h, VEC_GLA)

                def take():
                    dve.wait_ge(s_jobev, JOB_GROUPS + GROUP * (h + 1))
                    nc.vector.tensor_copy(taken, fresh).then_inc(s_take, 1)
                    dve.wait_ge(s_take, h + 1)
                    link(nc.vector.tensor_copy(bias, vec[:, bass.ds(h * 2 + V_BIAS, 2)]))
                    nc.vector.tensor_copy(up[:, :], gup[:, bass.ds(h * DK, DK)]).then_inc(s_up, 1)

                def gate_in(d):
                    dve.wait_ge(s_z, 2 * h + d + 1)
                    if d:
                        dve.wait_ge(s_qk, 6 * h + 3)
                    nc.vector.tensor_scalar(zb, psum[:, 2 + d], bias[:, d:d + 1], None, ALU.add).then_inc(s_zb, 1)

                def cumulate(d):
                    dve.wait_ge(s_ln, 2 * h + d + 1)
                    link(nc.vector.scalar_tensor_tensor(out=la, in0=zb, scalar=0.0, in1=ab, op0=ALU.min, op1=ALU.subtract))
                    scan = nc.vector.tensor_tensor_scan(cum, mask, la, 0.0, ALU.mult, ALU.add)
                    cum_c = cum.rearrange("p (n c) -> p n c", c=CHUNK)
                    exc_c, la_c = exc.rearrange("p (n c) -> p n c", c=CHUNK), la.rearrange("p (n c) -> p n c", c=CHUNK)
                    total = cum_c[:, :, CHUNK - 1:CHUNK].broadcast_to([P, NC, CHUNK])
                    if d == 0:
                        scan.then_inc(s_cum, 1)
                        dve.wait_ge(s_cum, 2 * h + 1)
                        nc.vector.tensor_tensor(exc_c, total, cum_c, ALU.subtract).then_inc(s_exc, 1)
                    else:
                        link(scan)
                        link(nc.vector.tensor_tensor(exc, cum, la, ALU.subtract))
                        nc.vector.tensor_tensor(la_c, total, exc_c, ALU.subtract).then_inc(s_cum, 1)

                def decayed(d):
                    dve.wait_ge(s_e, 6 * h + 3 * d + 1)
                    nc.vector.scalar_tensor_tensor(out=qd[:, d], in0=taken[:, 0], scalar=float(DK) ** -0.5, in1=zb,
                                                   op0=ALU.mult, op1=ALU.mult).then_inc(s_qk, 1)
                    dve.wait_ge(s_e, 6 * h + 3 * d + 2)
                    nc.vector.tensor_tensor(kd[:, d], taken[:, 1], ab, ALU.mult).then_inc(s_qk, 1)
                    dve.wait_ge(s_e, 6 * h + 3 * d + 3)
                    if d:
                        dve.wait_ge(s_ktp, 2 * h + 1)
                    nc.vector.tensor_tensor(ke, taken[:, 1], exc, ALU.mult).then_inc(s_qk, 1)

                def states(n0, n1):
                    for n in range(n0, n1):
                        d, step = n % 2, n // 2
                        c = step if d == 0 else NC - 1 - step
                        to = c + 1 if d == 0 else c - 1
                        dve.wait_ge(s_kv, 14 * h + n + 1)
                        new, got = state[:, to, DV * d:DV * (d + 1)], psum[:, KV_BANKS[n % 4], 0:DV]
                        if step == 0:
                            if n == 0:
                                dve.wait_ge(s_dec, 2 * h + 2)
                            nc.vector.tensor_copy(new, got).then_inc(s_st, 1)
                        else:
                            dve.wait_ge(s_st, 14 * h + n - 1)
                            nc.vector.scalar_tensor_tensor(out=new, in0=state[:, c, DV * d:DV * (d + 1)],
                                                           scalar=dec[:, d, c:c + 1], in1=got, op0=ALU.mult,
                                                           op1=ALU.add).then_inc(s_st, 1)

                def add_scores():
                    dve.wait_ge(s_atm, 4 * h + 4)
                    for half in range(2):
                        r = slice(64 * half, 64 * half + 64)
                        nc.vector.tensor_tensor(at_sum[r, :, CHUNK * half:CHUNK * (half + 1)], at[r, 0], at[r, 1], ALU.add
                                                ).then_inc(s_ats, 1)

                def gate_rms():
                    dve.wait_ge(s_oss, h + 1)
                    inverse(psum[:, 2], DV, g_ri, s_ginv)

                def gated():
                    dve.wait_ge(s_gr, h + 1)
                    dve.wait_ge(s_sil, h + 1)
                    for t in range(DVT):
                        link(nc.vector.scalar_tensor_tensor(out=osq[:, t], in0=psum[:, 5 + t], scalar=vec[:, V_GLA + t:V_GLA + t + 1],
                                                            in1=g_r, op0=ALU.mult, op1=ALU.mult))
                        nc.vector.tensor_tensor(cur[:, bass.ds(2 * h + t, 1)].rearrange("p o t -> p (o t)"), osq[:, t], sil[:, t],
                                                ALU.mult).then_inc(s_y, 1)

                at_part = {0: lambda: (take(), gate_in(0)), 2: lambda: (cumulate(0), decayed(0)), 4: lambda: gate_in(1),
                           5: lambda: (cumulate(1), decayed(1)),
                           8: lambda: states(0, 4), 9: lambda: states(4, 8), 10: lambda: (add_scores(), states(8, 12)),
                           11: lambda: states(12, 14), 15: gate_rms, 16: gated}
                for p in range(PARTS):
                    if p == 0:
                        at_part[p]()
                    if p % 3 == 0:
                        rest(job(JOB_GROUPS + GROUP + 1, GROUP, h, p // 3))
                    if p in at_part and p:
                        at_part[p]()
                dve.wait_ge(s_y, 2 * h + 2)
                link.leave(NGLA)

            def attention(g, first, i, jobs):
                def take():
                    dve.wait_ge(s_jobev, GROUP * (NGLA + g + 1) + JOB_GROUPS)
                    q_in, q_out = fresh.rearrange("p (r j) t -> p r j t", j=3), taken.rearrange("p (r j) t -> p r j t", j=3)
                    link(nc.vector.tensor_scalar(q_out[:, :, 0], q_in[:, :, 0], float(HD) ** -0.5, None, ALU.mult))
                    nc.vector.tensor_copy(q_out[:, :, 1:3], q_in[:, :, 1:3]).then_inc(s_take, 1)
                    link(nc.vector.tensor_copy(slope, vec[:, bass.ds(g * 4 + V_SLOPE, 4)]))
                    for pr in range(2):
                        dve.wait_ge(s_avp, 2 * g + pr + 1)
                        nc.vector.tensor_copy(va[:, pr, :, :, 0:HD], psum[:, 7 - pr].rearrange("p (s h e) -> p s h e", h=2, e=HD)
                                              ).then_inc(s_av, 1)

                def out_tile(pr):
                    dve.wait_ge(s_otp, 2 * g + pr + 1)
                    nc.vector.tensor_copy(cur[:, bass.ds(2 * g + (8 + pr), 1)].rearrange("p o t -> p (o t)"), psum[:, 7]
                                          ).then_inc(s_ot, 1)

                for p in range(PARTS):
                    if p == 0:
                        take()
                    if jobs and p % 3 == 0:
                        rest(job(first + 1, GROUP, i, p // 3))
                    n = p - PAIR_PART
                    if not jobs and 0 <= n < 2 * NPAIR and n % 2 == 0:
                        rest(job(JOB_OUT + 1, 0, 0, n // 2))
                    if p < 16:
                        hd, a = p // 4, p % 4
                        dve.wait_ge(s_qkm, 16 * g + p + 1)
                        if p >= 2:
                            dve.wait_ge(s_p, 16 * g + p - 1)
                            dve.wait_ge(s_sb, 16 * g + p - 1)
                        link(nc.vector.scalar_tensor_tensor(out=logit[:, p % 2], in0=dist_t[:, a], scalar=slope[:, hd:hd + 1],
                                                            in1=psum[:, 2 + p % 2], op0=ALU.mult, op1=ALU.add))
                        nc.vector.tensor_reduce(negmax[:, p % 2:p % 2 + 1], logit[:, p % 2], AX.X, ALU.max, negate=True
                                                ).then_inc(s_sb, 1)
                    if 1 <= p <= 16:
                        u = p - 1
                        dve.wait_ge(s_ptp, 16 * g + u + 1)
                        if u >= 2:
                            dve.wait_ge(s_pv, 16 * g + u - 1)
                        nc.vector.tensor_tensor(prob_t[:, u % 2].rearrange("p (s t) -> p s t", t=P),
                                                psum[:, 4 + u % 2].rearrange("p (s t) -> p s t", t=P),
                                                count_t[:, :, (u % 4) * P:(u % 4 + 1) * P], ALU.mult).then_inc(s_pt, 1)
                    if p == 10:
                        out_tile(0)
                    if not jobs:
                        if p in Y_SQUARES:
                            add_square(1, KD + Y_SQUARES.index(p), Y_SQUARES.index(p) % 2)
                        for k in range(HK):
                            if Y_HALVES[k] == p:
                                low(1, k, cur[:, k])
                    if p >= 2:
                        u = p - 2
                        hd = (u // 4) % 2
                        dve.wait_ge(s_pv, 16 * g + u + 1)
                        if u:
                            dve.wait_ge(s_nrm, 16 * g + u)
                        o = psum[:, 6, (u % 2) * P:(u % 2) * P + HD + 1]
                        link(nc.vector.reciprocal(rden, o[:, HD:HD + 1]))
                        nc.vector.tensor_scalar(att_rows[:, u % 4, HD * hd:HD * (hd + 1)], o[:, 0:HD], rden, None, ALU.mult
                                                ).then_inc(s_nrm, 1)
                dve.wait_ge(s_nrm, 16 * g + 16)
                out_tile(1)

            dve.wait_ge(s_tab, 32)
            link(nc.vector.tensor_copy(count_t, work[:, 12:16]))
            link(nc.vector.memset(va[:, :, :, :, HD:HD + 1], 1.0))
            first = JOB_GROUPS + GROUP * (NGLA + 1)
            with dve.Fori(0, NATT - 1) as g:
                link.enter(g, VEC_ATT)
                attention(g, first, g, True)
                link.leave(NATT - 1)
            attention(NATT - 1, 0, 0, False)

            add_square(1, KD + 7, 1)
            rest(job(JOB_WHOLE + 1, 0, 0, 0))
            rms(1, 8 * P)
            normed(1, 8, V_ATT, KD)
            for n in range(2):
                rest(job(JOB_WHOLE + 2, 0, 0, n))
                dve.wait_ge(s_jobmm, JOB_WHOLE + n + 1)
                dve.wait_ge(s_xr[n], 16)
                nc.vector.tensor_tensor(cur[:, 2 * NPAIR + n], psum[:, n], x_res[:, n], ALU.add).then_inc(s_jobev, 1)
                add_square(2, SQ_BASE[2] + n, n)
            for a in range(NPAIR):
                if a:
                    rest(job(JOB_ATT + 1, 0, 0, a))
                for j in range(2):
                    m = 2 * a + j
                    if j == 0:
                        dve.wait_ge(s_half, NPAIR + a + 1)
                    else:
                        dve.wait_ge(s_jobmm, JOB_ATT + a + 1)
                    dve.wait_ge(s_xr[j], 16 * (a + 2))
                    link(nc.vector.tensor_tensor(x_res[:, j], psum[:, j], x_res[:, j], ALU.add))
                    nc.vector.tensor_tensor(cur[:, m], x_res[:, j], partial[m], ALU.add).then_inc(s_jobev if j else s_halfev, 1)
                    add_square(2, SQ_BASE[2] + 2 + m, j)
            rms(2, D)
            normed(2, 0, V_N2, KD + 8)
            with dve.Fori(0, PEER_HEADS) as i:
                for j in range(2):
                    rest(job(JOB_Q + 1, 2, i, j))

            def apart():
                dve.sem_inc(s_apart, 1)

            def sixteen(values, cut, best, where):
                apart()
                link(nc.vector.max(best[:, 0:8], values))
                apart()
                link(nc.vector.max_index(where[:, 0:8], best[:, 0:8], values))
                apart()
                link(nc.vector.match_replace(cut, best[:, 0:8], values, LOW))
                apart()
                link(nc.vector.max(best[:, 8:16], cut))
                apart()
                link(nc.vector.max_index(where[:, 8:16], best[:, 8:16], cut))

            def top_keys(i, u):
                link(nc.vector.tensor_copy(tk_in.rearrange("p c k -> p (c k)"), score_t[:, bass.ds(512 * i + 256 * u, 256)]))
                for c in range(2):
                    sixteen(tk_in[:, c], tk_cut[:, c], val[:, c], idx[:, c])

            def top_pairs(i, u):
                sums = pair_sum.rearrange("p (a b) -> p a b", b=TOPK)
                link(nc.vector.tensor_tensor(sums, val[:, 0].unsqueeze(2).broadcast_to([P, TOPK, TOPK]),
                                             val[:, 1].unsqueeze(1).broadcast_to([P, TOPK, TOPK]), ALU.add))
                sixteen(pair_sum, pair_cut, top[:, u], place)
                nc.vector.tensor_scalar(tk_neg[:, u:u + 1], top[:, u, 0:1], -1.0, None, ALU.mult).then_inc(s_tke, 1)
                link(nc.vector.tensor_single_scalar(place_2[:, 0], place, 4, ALU.logical_shift_right))
                link(nc.vector.tensor_single_scalar(place_2[:, 1], place, TOPK - 1, ALU.bitwise_and))
                link(nc.vector.tensor_copy(place_f, place_2))
                link(nc.vector.tensor_copy(idx_f, idx))
                for c in range(2):
                    link(nc.vector.tensor_tensor(picked, place_f[:, c].unsqueeze(2).broadcast_to([P, TOPK, TOPK]),
                                                 count_up[:, 0:TOPK].unsqueeze(1).broadcast_to([P, TOPK, TOPK]), ALU.is_equal))
                    link(nc.vector.tensor_tensor(chosen, picked, idx_f[:, c].unsqueeze(1).broadcast_to([P, TOPK, TOPK]), ALU.mult))
                    nc.vector.tensor_reduce(routed[:, 1 + c, bass.ds(32 * i + 16 * u, TOPK)], chosen, AX.X, ALU.add
                                            ).then_inc(s_route, 1)
                    dve.wait_ge(s_route, 6 * i + 2 * u + c + 1)

            def gates_of(i):
                for u in range(2):
                    dve.wait_ge(s_tkx, 2 * i + u + 1)
                    link(nc.vector.reciprocal(tk_inv[:, u:u + 1], tk_sum[:, u:u + 1]))
                    nc.vector.tensor_scalar(routed[:, 0, bass.ds(32 * i + 16 * u, TOPK)], top_exp[:, u], tk_inv[:, u:u + 1], None,
                                            ALU.mult).then_inc(s_route, 1)

            dve.wait_ge(s_sc, 2 * PEER_HEADS)
            dve.wait_ge(s_keys, 32)
            with dve.Fori(0, U1) as i:
                link.enter(i, VEC_TOP)
                for j in range(4):
                    rest(job(JOB_U + 1, 4, i, j))
                    (top_keys, top_pairs)[j % 2](i, j // 2)
                gates_of(i)
                dve.wait_ge(s_route, 6 * i + 6)
                link.leave(U1)

            def hot(i, r, q):
                n = 16 * i + 8 * r + q
                dve.wait_ge(s_gmm, n - 1 + HOT_FREE)
                for t in range(4):
                    col = slice(4 * q + t, 4 * q + t + 1)
                    nc.vector.tensor_scalar(hot2[:, 4 * (q % 2) + t], count_up, route_tb[:, r, 2, col], None, ALU.is_equal)
                    last = nc.vector.tensor_scalar(hot1[:, 4 * (q % 2) + t], count_up, route_tb[:, r, 1, col],
                                                   route_tb[:, r, 0, col], ALU.is_equal, ALU.mult)
                last.then_inc(s_hot, 1)

            dve.wait_ge(s_rt, 3)

            def u2_round(i, last=False):
                for r in range(2):
                    link(nc.vector.tensor_copy(route_tb[:, r], routed_t[:, :, bass.ds(2 * TB * i + TB * r, TB)]))
                    for j in range(4):
                        hot(i, r, 2 * j)
                        hot(i, r, 2 * j + 1)
                        if not (last and r == 1 and j == 3):
                            rest(job(JOB_U + 4 * U1 + 1, 8, i, 4 * r + j))
                    dve.wait_ge(s_hot, 16 * i + 8 * r + 8)

            with dve.Fori(0, U2 // 2 - 1) as i:
                link.enter(i, 2)
                u2_round(i)
                link.leave(U2 // 2 - 1)
            u2_round(U2 // 2 - 1, last=True)

            dve.wait_ge(s_gev, 8 * U2 + BANKS_FREE)
            link(nc.vector.tensor_copy(g_t[0][:, U2 - 1], gate_t[:, 1, 0:VG]))

            def v_rest(half, i, r, e, early=False):
                n = NKEYS * half + 8 * i + 4 * r + e
                if e == 0:
                    dve.wait_ge(s_g[r], 16 * (i + (16 * half + 1)))
                dve.wait_ge(s_a[e], 16 * (2 * i + (32 * half + r + 1)))
                if not (early and r == 0 and e < 2):
                    dve.wait_ge(s_wh, n - 1)
                    dve.wait_ge(s_wl, n - 1)
                nc.vector.tensor_tensor(weight_t[:, e % 2].rearrange("p (b t) -> p b t", t=TB), g_t[r][:, :, e],
                                        a_t[:, e].rearrange("p (b t) -> p b t", t=TB), ALU.mult).then_inc(s_w, 1)
                dve.wait_ge(s_vh, n + 1)
                nc.vector.tensor_tensor(v_lo[:, e], v_raw[:, e], v_hi[:, e].bitcast(F32), ALU.subtract).then_inc(s_vl, 1)
                dve.wait_ge(s_wh, n + 1)
                nc.vector.tensor_tensor(g_lo[:, e], weight_t[:, e % 2], g_hi[:, e].bitcast(F32), ALU.subtract).then_inc(s_wl, 1)

            for half in range(2):
                for r in range(2):
                    for e in range(VG):
                        if not (half and r == e == 0):
                            v_rest(half, 0, r, e, half == 0)
                        if half:
                            m = VG * r + e
                            add_square(3, SQ_BASE[3] + m, m % 2)
                with dve.Fori(1, VR // 2) as i:
                    for r in range(2):
                        for e in range(VG):
                            v_rest(half, i, r, e)
                if half == 0:
                    v_rest(1, 0, 0, 0)
                dve.wait_ge(s_hl, 32)
                for m in range(HT):
                    if m < HT - 1:
                        dve.wait_ge(s_vend, (HT - 1) * half + m + 1)
                    else:
                        dve.wait_ge(s_vmm, NKEYS * (half + 1))
                    nc.vector.tensor_tensor(cur[:, HT * half + m], cur[:, HT * half + m], psum[:, m], ALU.add).then_inc(s_vev, 1)
                    if half and m:
                        add_square(3, SQ_BASE[3] + HT + m - 1, (m - 1) % 2)
            add_square(3, SQ_BASE[3] + KD - 1, 1)
            rms(3, D)
            for k in range(KD):
                nc.vector.scalar_tensor_tensor(out=cur[:, k], in0=cur[:, k], scalar=vec[:, V_NF + k:V_NF + k + 1], in1=r_t[3],
                                               op0=ALU.mult, op1=ALU.mult).then_inc(s_fin, 1)


def weight_tiles(w):
    n = w.shape[1] // P
    return w.reshape(KD, P, n, P).transpose(2, 1, 0, 3).reshape(n, P, KD * P)


def constants():
    t = np.arange(T)
    gap = np.abs(t[:, None] - t[None, :])
    reached = [(gap % r == 0) & (gap <= w // 2) for w, r in PATTERNS]
    count = sum(x.astype(np.float32) for x in reached)
    dist = np.where(count > 0, -gap, NEG).astype(np.float32)
    tiles = lambda a: np.ascontiguousarray(a.reshape(TT, P, T).transpose(1, 0, 2))
    mask = np.tile((t % CHUNK != 0).astype(np.float32), (P, 1))
    steps = np.tile(np.arange(P, dtype=np.float32), (P, 1))
    return tiles(dist), tiles(count), np.eye(P, dtype=np.float32), mask, steps


def layout(a):
    w_in = a["w_in"][0]
    qk, vg, att = GLA_HEADS * DK, GLA_HEADS * DV, ATT_HEADS * HD
    at = np.cumsum([0, qk, qk, vg, vg, RANK, RANK, att, att, att])
    gq, gk, gv, gr, gf, gb, aq, ak, av = [w_in[:, at[n]:at[n + 1]] for n in range(9)]
    gate = np.zeros((D, P), np.float32)
    gate[:, 0:RANK], gate[:, 32:32 + RANK] = gf, gb
    cols = [gate]
    for h in range(GLA_HEADS):
        k, v = slice(DK * h, DK * (h + 1)), slice(DV * h, DV * (h + 1))
        cols += [gq[:, k], gk[:, k], gv[:, v], gr[:, v]]
    for h in range(ATT_HEADS // 2):
        c = slice(P * h, P * (h + 1))
        cols += [aq[:, c], ak[:, c], av[:, c]]
    cols += [a["w_out"][0], a["peer_w_q"][0], a["peer_u"][0].T]
    w_out, *rest = [weight_tiles(c) for c in cols[-3:]]
    pairs = w_out[:2 * NPAIR].reshape(NPAIR, 2, P, 2, HK * P).transpose(3, 0, 2, 1, 4).reshape(2, NPAIR, P, KD * P)
    weights = np.concatenate([weight_tiles(np.concatenate(cols[:1 + 4 * GLA_HEADS + 3 * ATT_HEADS // 2], axis=1)),
                              pairs[0], w_out[2 * NPAIR:], pairs[1], *rest])
    col = lambda v: v.reshape(-1, P).T
    bias = np.stack([a["gla_gate_bias_f"][0].reshape(GLA_HEADS, DK), a["gla_gate_bias_b"][0].reshape(GLA_HEADS, DK)], 1)
    slopes = np.tile((2.0 ** (-8.0 * np.arange(1, ATT_HEADS + 1) / ATT_HEADS)).astype(np.float32), (P, 1))
    vectors = np.concatenate([col(a["norm1_g"][0]), col(a["norm2_g"][0]), col(a["final_norm_g"]), col(a["att_norm_g"][0]),
                              col(a["gla_norm_g"][0]), bias.reshape(-1, P).T, slopes], axis=1)
    gate_up = np.zeros((32 + RANK, qk), np.float32)
    gate_up[0:RANK], gate_up[32:] = a["gla_gate_up_f"][0], a["gla_gate_up_b"][0]
    dist, count, ident, mask, steps = constants()
    return {
        "x_t": np.ascontiguousarray(a["x"][0].T.reshape(KD, P, T).transpose(1, 0, 2)),
        "weights": weights,
        "peer_v": a["peer_v"][0],
        "sub_keys": np.ascontiguousarray(a["peer_sub_keys"][0].reshape(2 * PEER_HEADS, NKEYS, P).transpose(2, 0, 1)),
        "vectors": np.ascontiguousarray(vectors), "gate_up": gate_up,
        "dist": dist, "count": count, "ident": ident, "scan_mask": mask, "steps": steps,
    }


def kernel(**inputs):
    import concourse.bacc as bacc
    from concourse.bass_utils import run_bass_kernel_spmd

    nc = bacc.Bacc("TRN2", target_bir_lowering=False, num_devices=1)
    arrays = layout({k: np.asarray(v) for k, v in inputs.items()})
    args = [nc.dram_tensor(n, a.shape, mybir.dt.from_np(a.dtype), kind="ExternalInput").ap() for n, a in arrays.items()]
    out_t = nc.dram_tensor("out_t", (D, T), F32, kind="ExternalOutput").ap()
    layer(nc, *args, out_t)
    r = run_bass_kernel_spmd(nc, [arrays], core_ids=[0])
    return np.ascontiguousarray(r.results[0]["out_t"].T).reshape(1, T, D)
```
